# Optimizing a Trainium2 kernel written in Bass

```python
import math
import jax, jax.numpy as jnp
from jax import lax
import numpy as np

D_MODEL = 1024
BATCH = 1
SEQ = 256
DEPTH = 1

N_HEADS_A = 8
HEAD_DIM = 64
WIDTH_A = N_HEADS_A * HEAD_DIM
IDX_HEADS = 8
IDX_DIM = 64
TOPK_MAX = 256
N_HEADS_B = 8
WIDTH_B = N_HEADS_B * HEAD_DIM
N_BUCKETS = 32
MAX_DISTANCE = 128
PEER_HEADS = 8
N_KEYS = 128
N_EXPERTS = N_KEYS * N_KEYS
PEER_QDIM = 256
PEER_HALF = PEER_QDIM // 2
PEER_TOPK = 16
Q_BLOCK = 128
TOK_CHUNK = 128
EPS = 1e-6
IN_SPLIT_SIZES = (WIDTH_A, WIDTH_A, WIDTH_A,
                  IDX_HEADS * IDX_DIM, IDX_DIM, IDX_HEADS,
                  WIDTH_B, WIDTH_B, WIDTH_B,
                  D_MODEL, D_MODEL)
IN_WIDTH = 3 * WIDTH_A + IDX_HEADS * IDX_DIM + IDX_DIM + IDX_HEADS + 3 * WIDTH_B + 2 * D_MODEL


def rmsnorm(x, g):
    xf = x.astype(jnp.float32)
    y = xf * lax.rsqrt(jnp.mean(xf * xf, axis=-1, keepdims=True) + EPS)
    return (y * g.astype(jnp.float32)).astype(x.dtype)

def modulate(h, shift, scale):
    return h * (1 + scale[:, None, :]) + shift[:, None, :]

def t5_bucket(n):
    max_exact = N_BUCKETS // 2
    nf = jnp.maximum(n, 1).astype(jnp.float32)
    large = max_exact + (jnp.log(nf / max_exact) / math.log(MAX_DISTANCE / max_exact)
                         * (N_BUCKETS - max_exact)).astype(jnp.int32)
    large = jnp.minimum(large, N_BUCKETS - 1)
    return jnp.where(n < max_exact, n, large)

def to_blocks(a, nblk):
    b = a.shape[0]
    return a.reshape(b, nblk, Q_BLOCK, *a.shape[2:]).swapaxes(0, 1)

def dsa_attention(q, k, v, qi, ki, wi, rel_bias):
    b, s, h, dh = q.shape
    topk = min(TOPK_MAX, s // 4)
    nblk = s // Q_BLOCK
    key_pos = jnp.arange(s)
    idx_scale = (IDX_DIM ** -0.5) * (IDX_HEADS ** -0.5)

    def one_block(args):
        blk, qb, qib, wib = args
        q_pos = blk * Q_BLOCK + jnp.arange(Q_BLOCK)
        rel = jax.nn.relu(jnp.einsum('bthd,bsd->bths', qib, ki))
        score = jnp.einsum('bths,bth->bts', rel, wib).astype(jnp.float32) * idx_scale
        causal = key_pos[None, :] <= q_pos[:, None]
        score = jnp.where(causal[None], score, -jnp.inf)
        top_score, idx = lax.top_k(score, topk)
        valid = jnp.isfinite(top_score)
        kg = jax.vmap(lambda kk, ii: kk[ii])(k, idx)
        vg = jax.vmap(lambda vv, ii: vv[ii])(v, idx)
        logits = jnp.einsum('bthd,btkhd->bhtk', qb, kg).astype(jnp.float32) * (dh ** -0.5)
        bias = rel_bias[t5_bucket(q_pos[None, :, None] - idx)].astype(jnp.float32)
        logits = logits + jnp.moveaxis(bias, -1, 1)
        logits = jnp.where(valid[:, None], logits, -jnp.inf)
        p = jax.nn.softmax(logits, axis=-1).astype(v.dtype)
        return jnp.einsum('bhtk,btkhd->bthd', p, vg)

    out = lax.map(one_block, (jnp.arange(nblk), to_blocks(q, nblk), to_blocks(qi, nblk), to_blocks(wi, nblk)))
    return out.swapaxes(0, 1).reshape(b, s, h * dh)

def stick_breaking_attention(q, k, v):
    b, s, h, dh = q.shape
    nblk = s // Q_BLOCK
    key_pos = jnp.arange(s)

    def one_block(args):
        blk, qb = args
        q_pos = blk * Q_BLOCK + jnp.arange(Q_BLOCK)
        z = jnp.einsum('bthd,bshd->bhts', qb, k).astype(jnp.float32) * (dh ** -0.5)
        strict = (key_pos[None, :] < q_pos[:, None])[None, None]
        log_beta = jax.nn.log_sigmoid(z)
        log_one_minus = jnp.where(strict, log_beta - z, 0.0)
        suffix = lax.cumsum(log_one_minus, axis=3, reverse=True) - log_one_minus
        a = jnp.where(strict, jnp.exp(log_beta + suffix), 0.0).astype(v.dtype)
        return jnp.einsum('bhts,bshd->bthd', a, v)

    out = lax.map(one_block, (jnp.arange(nblk), to_blocks(q, nblk)))
    return out.swapaxes(0, 1).reshape(b, s, h * dh)

def peer_ffn(h, w_q, sub_keys, u, v):
    t, d = h.shape
    qh = (h @ w_q).reshape(t, PEER_HEADS, 2, PEER_HALF)
    s = jnp.einsum('thcd,hcnd->thcn', qh, sub_keys).astype(jnp.float32)
    s1, i1 = lax.top_k(s[:, :, 0], PEER_TOPK)
    s2, i2 = lax.top_k(s[:, :, 1], PEER_TOPK)
    cand = (s1[..., :, None] + s2[..., None, :]).reshape(t, PEER_HEADS, PEER_TOPK * PEER_TOPK)
    cand_idx = (i1[..., :, None] * N_KEYS + i2[..., None, :]).reshape(t, PEER_HEADS, PEER_TOPK * PEER_TOPK)
    top_s, pos = lax.top_k(cand, PEER_TOPK)
    eidx = jnp.take_along_axis(cand_idx, pos, axis=-1)
    g = jax.nn.softmax(top_s, axis=-1)
    nchunk = t // TOK_CHUNK

    def one_chunk(args):
        hc, ec, gc = args
        pre = jnp.einsum('cd,chkd->chk', hc, u[ec]).astype(jnp.float32)
        coef = (gc * jax.nn.gelu(pre, approximate=False)).astype(h.dtype)
        return jnp.einsum('chk,chkd->cd', coef, v[ec])

    out = lax.map(one_chunk, (h.reshape(nchunk, TOK_CHUNK, d),
                              eidx.reshape(nchunk, TOK_CHUNK, PEER_HEADS, PEER_TOPK),
                              g.reshape(nchunk, TOK_CHUNK, PEER_HEADS, PEER_TOPK)))
    return out.reshape(t, d)

def first_inputs(seed: int = 0) -> dict:
    key = jax.random.key(seed)
    ks = jax.random.split(key, 20)
    D = D_MODEL
    nrm = jax.random.normal
    x = nrm(ks[0], (BATCH, SEQ, D), jnp.float32)
    c = nrm(ks[1], (BATCH, D), jnp.float32)
    w_ada = nrm(ks[2], (DEPTH, D, 6 * D), jnp.float32) * (0.5 * D ** -0.5)
    b_ada = nrm(ks[3], (DEPTH, 6 * D), jnp.float32) * 0.01
    norm1_g = 1.0 + 0.05 * nrm(ks[4], (DEPTH, D), jnp.float32)
    norm2_g = 1.0 + 0.05 * nrm(ks[5], (DEPTH, D), jnp.float32)
    w_in = nrm(ks[6], (DEPTH, D, IN_WIDTH), jnp.float32) * D ** -0.5
    rel_bias = nrm(ks[7], (N_BUCKETS, N_HEADS_A), jnp.float32) * 0.5
    w_proj_a = nrm(ks[8], (DEPTH, WIDTH_A, D), jnp.float32) * WIDTH_A ** -0.5
    w_proj_b = nrm(ks[9], (DEPTH, WIDTH_B, D), jnp.float32) * WIDTH_B ** -0.5
    w_out = nrm(ks[10], (DEPTH, D, D), jnp.float32) * D ** -0.5
    peer_wq = nrm(ks[11], (DEPTH, D, PEER_HEADS * PEER_QDIM), jnp.float32) * D ** -0.5
    peer_sub_keys = nrm(ks[12], (DEPTH, PEER_HEADS, 2, N_KEYS, PEER_HALF), jnp.float32) * PEER_HALF ** -0.5
    peer_u = nrm(ks[13], (DEPTH, N_EXPERTS, D), jnp.float32) * D ** -0.5
    peer_v = nrm(ks[14], (DEPTH, N_EXPERTS, D), jnp.float32) * PEER_HEADS ** -0.5
    final_g = 1.0 + 0.05 * nrm(ks[15], (D,), jnp.float32)
    return {"x": x, "c": c, "w_ada": w_ada, "b_ada": b_ada, "norm1_g": norm1_g, "norm2_g": norm2_g,
            "w_in": w_in, "rel_bias": rel_bias, "w_proj_a": w_proj_a, "w_proj_b": w_proj_b,
            "w_out": w_out, "peer_wq": peer_wq, "peer_sub_keys": peer_sub_keys, "peer_u": peer_u,
            "peer_v": peer_v, "final_g": final_g}

def first_block(x, c, w_ada, b_ada, norm1_g, norm2_g, w_in, rel_bias, w_proj_a, w_proj_b, w_out,
              peer_wq, peer_sub_keys, peer_u, peer_v, final_g):
    b, s, d = x.shape
    offsets = []
    acc = 0
    for size in IN_SPLIT_SIZES[:-1]:
        acc += size
        offsets.append(acc)
    cond = jax.nn.silu(c)
    for l in range(DEPTH):
        mod = (cond @ w_ada[l] + b_ada[l]).reshape(b, 6, d)
        shift1, scale1, gate1, shift2, scale2, gate2 = [mod[:, i] for i in range(6)]

        hn = modulate(rmsnorm(x, norm1_g[l]), shift1, scale1)
        proj = hn @ w_in[l]
        qa, ka, va, qi, ki, wi, qb, kb, vb, ga, gb = jnp.split(proj, offsets, axis=-1)
        hd = (b, s, -1, HEAD_DIM)
        ya = dsa_attention(qa.reshape(hd), ka.reshape(hd), va.reshape(hd),
                           qi.reshape(b, s, IDX_HEADS, IDX_DIM), ki, wi, rel_bias)
        yb = stick_breaking_attention(qb.reshape(hd), kb.reshape(hd), vb.reshape(hd))
        merged = jax.nn.sigmoid(ga) * (ya @ w_proj_a[l]) + jax.nn.sigmoid(gb) * (yb @ w_proj_b[l])
        x = x + gate1[:, None, :] * (merged @ w_out[l])

        hn2 = modulate(rmsnorm(x, norm2_g[l]), shift2, scale2)
        f = peer_ffn(hn2.reshape(b * s, d), peer_wq[l], peer_sub_keys[l], peer_u[l], peer_v[l]).reshape(b, s, d)
        x = x + gate2[:, None, :] * f
    return rmsnorm(x, final_g)


N_META = 16
NORM_EPS = 1e-6
SSM_WIDTH = D_MODEL // 2
SSM_GROUP = 16
SSM_GROUPS = SSM_WIDTH // SSM_GROUP
SSM_STATE = 64
ML_WIDTH = D_MODEL
ML_HEADS = 4
ML_HEAD_DIM = ML_WIDTH // ML_HEADS
ML_CHUNK = 64
ML_CONV = 4
ML_QKV_BLOCK = 4
PEER_NKEYS = 128
PEER_EXPERTS = PEER_NKEYS * PEER_NKEYS
PEER_HALF_2 = PEER_QDIM // 2
PEER_TOKEN_BLOCK = 256
IN_COLS = SSM_WIDTH + 2 * ML_WIDTH + 2 * D_MODEL


def rmsnorm_2(x, g):
    x32 = x.astype(jnp.float32)
    y = x32 * lax.rsqrt(jnp.mean(x32 * x32, axis=-1, keepdims=True) + NORM_EPS)
    return (y * g.astype(jnp.float32)).astype(x.dtype)

def s5_branch(u, a_re, a_im, log_dt, b_re, b_im, c_re, c_im, d, w_glu, b_glu):
    f32 = jnp.float32
    bn, L, _ = u.shape
    u32 = u.astype(f32).reshape(bn, L, SSM_GROUPS, SSM_GROUP)
    lam = lax.complex(a_re.astype(f32), a_im.astype(f32))
    dt = jnp.exp(log_dt.astype(f32))[:, None]
    a_bar = jnp.exp(lam * dt)
    b_bar = ((a_bar - 1.0) / lam)[..., None] * lax.complex(b_re.astype(f32), b_im.astype(f32))
    bu = jnp.einsum('blgc,gpc->blgp', u32.astype(jnp.complex64), b_bar)
    a_seq = jnp.broadcast_to(a_bar, (1, L) + a_bar.shape)

    def combine(e1, e2):
        a1, b1 = e1
        a2, b2 = e2
        return a1 * a2, a2 * b1 + b2

    _, states = lax.associative_scan(combine, (a_seq, bu), axis=1)
    c = lax.complex(c_re.astype(f32), c_im.astype(f32))
    y = jnp.real(jnp.einsum('blgp,gcp->blgc', states, c)) + d.astype(f32).reshape(SSM_GROUPS, SSM_GROUP) * u32
    y = jax.nn.gelu(y.reshape(bn, L, SSM_WIDTH))
    y = y * jax.nn.sigmoid(y @ w_glu.astype(f32) + b_glu.astype(f32))
    return y.astype(u.dtype)

def causal_depthwise_conv(x, w, b):
    K = w.shape[0]
    L = x.shape[1]
    xp = jnp.pad(x, ((0, 0), (K - 1, 0), (0, 0)))
    return sum(xp[:, j:j + L] * w[j] for j in range(K)) + b

def blockdiag(x, w):
    sh = x.shape
    xb = x.reshape(sh[:-1] + (w.shape[0], w.shape[1]))
    return jnp.einsum('blnc,ncd->blnd', xb, w).reshape(sh)

def mlstm_chunk_step(carry, xs):
    c_mat, n_vec, m_st = carry
    q, k, v, log_i, log_f = xs
    b = jnp.cumsum(log_f, axis=-1)
    g = b[..., -1]
    causal = jnp.tril(jnp.ones((ML_CHUNK, ML_CHUNK), dtype=bool))
    d_log = jnp.where(causal, b[..., :, None] - b[..., None, :] + log_i[..., None, :], -jnp.inf)
    inter_log = b + m_st[..., None]
    m_t = jnp.maximum(inter_log, jnp.max(d_log, axis=-1))
    w_intra = jnp.exp(d_log - m_t[..., None])
    s = jnp.einsum('bhtd,bhsd->bhts', q, k) * w_intra
    w_inter = jnp.exp(inter_log - m_t)
    num = jnp.einsum('bhts,bhsd->bhtd', s, v) + w_inter[..., None] * jnp.einsum('bhed,bhtd->bhte', c_mat, q)
    den = jnp.sum(s, axis=-1) + w_inter * jnp.einsum('bhd,bhtd->bht', n_vec, q)
    h = num / jnp.maximum(jnp.abs(den), jnp.exp(-m_t))[..., None]
    a = g[..., None] - b + log_i
    m_new = jnp.maximum(g + m_st, jnp.max(a, axis=-1))
    w_state = jnp.exp(a - m_new[..., None])
    decay = jnp.exp(g + m_st - m_new)
    c_new = decay[..., None, None] * c_mat + jnp.einsum('bhs,bhse,bhsd->bhed', w_state, v, k)
    n_new = decay[..., None] * n_vec + jnp.einsum('bhs,bhsd->bhd', w_state, k)
    return (c_new, n_new, m_new), h

def mlstm_branch(xm, z, conv_w, conv_b, wq, wk, wv, w_if, b_if, norm_g, skip):
    f32 = jnp.float32
    bn, L, _ = xm.shape
    H, dh = ML_HEADS, ML_HEAD_DIM
    xc = jax.nn.silu(causal_depthwise_conv(xm, conv_w, conv_b))
    q = blockdiag(xc, wq)
    k = blockdiag(xc, wk)
    v = blockdiag(xm, wv)
    gates = (jnp.concatenate([q, k, v], axis=-1) @ w_if + b_if).astype(f32)
    log_i = gates[..., :H]
    log_f = jax.nn.log_sigmoid(gates[..., H:])
    k = k * (dh ** -0.5)
    pad_f = (-N_META) % ML_CHUNK
    pad_b = (-(L + pad_f)) % ML_CHUNK
    n_chunks = (L + pad_f + pad_b) // ML_CHUNK

    def heads_to_chunks(t):
        t = jnp.pad(t.astype(f32).reshape(bn, L, H, dh), ((0, 0), (pad_f, pad_b), (0, 0), (0, 0)))
        return t.reshape(bn, n_chunks, ML_CHUNK, H, dh).transpose(1, 0, 3, 2, 4)

    def gate_to_chunks(t):
        t = jnp.pad(t, ((0, 0), (pad_f, pad_b), (0, 0)))
        return t.reshape(bn, n_chunks, ML_CHUNK, H).transpose(1, 0, 3, 2)

    init = (jnp.zeros((bn, H, dh, dh), f32), jnp.zeros((bn, H, dh), f32), jnp.zeros((bn, H), f32))
    _, hc = lax.scan(mlstm_chunk_step, init,
                     (heads_to_chunks(q), heads_to_chunks(k), heads_to_chunks(v),
                      gate_to_chunks(log_i), gate_to_chunks(log_f)))
    h = hc.transpose(1, 0, 3, 2, 4).reshape(bn, n_chunks * ML_CHUNK, H, dh)[:, pad_f:pad_f + L]
    h = jax.nn.sigmoid(z.astype(f32)).reshape(bn, L, H, dh) * h
    h = h * lax.rsqrt(jnp.mean(h * h, axis=-1, keepdims=True) + NORM_EPS)
    h = h.reshape(bn, L, ML_WIDTH) * norm_g.astype(f32) + skip.astype(f32) * xc.astype(f32)
    return h.astype(xm.dtype)

def peer_ffn_2(xn, w_q, sub_keys, u_tab, v_tab):
    f32 = jnp.float32
    bn, L, D = xn.shape
    T = bn * L
    n_blk = -(-T // PEER_TOKEN_BLOCK)
    xt = jnp.pad(xn.reshape(T, D), ((0, n_blk * PEER_TOKEN_BLOCK - T), (0, 0)))
    xt = xt.reshape(n_blk, PEER_TOKEN_BLOCK, D)
    keys32 = sub_keys.astype(f32)

    def block(xb):
        q = (xb @ w_q).astype(f32).reshape(PEER_TOKEN_BLOCK, PEER_HEADS, 2, PEER_HALF_2)
        s = jnp.einsum('thid,hikd->thik', q, keys32)
        sv, si = lax.top_k(s, PEER_TOPK)
        cand = sv[..., 0, :, None] + sv[..., 1, None, :]
        cidx = si[..., 0, :, None] * PEER_NKEYS + si[..., 1, None, :]
        cand = cand.reshape(PEER_TOKEN_BLOCK, PEER_HEADS, PEER_TOPK * PEER_TOPK)
        cidx = cidx.reshape(PEER_TOKEN_BLOCK, PEER_HEADS, PEER_TOPK * PEER_TOPK)
        cs, ci = lax.top_k(cand, PEER_TOPK)
        eidx = jnp.take_along_axis(cidx, ci, axis=-1)
        gate = jax.nn.softmax(cs, axis=-1)
        ug = u_tab[eidx]
        act = jax.nn.gelu(jnp.einsum('td,thkd->thk', xb, ug).astype(f32))
        vg = v_tab[eidx]
        return jnp.einsum('thk,thkd->td', (gate * act).astype(vg.dtype), vg)

    out = lax.map(block, xt).reshape(n_blk * PEER_TOKEN_BLOCK, D)[:T]
    return out.reshape(bn, L, D).astype(xn.dtype)

def second_inputs(seed: int = 0) -> dict:
    key = jax.random.key(seed)
    ks = list(jax.random.split(key, 40))
    f32 = jnp.float32
    it = iter(ks)

    def nrm(shape, scale):
        return jax.random.normal(next(it), shape, f32) * scale

    def gain(shape):
        return 1.0 + nrm(shape, 0.02)

    Dp = DEPTH
    x = nrm((BATCH, SEQ, D_MODEL), 1.0)
    meta_tokens = nrm((N_META, D_MODEL), 1.0)
    norm1_g = gain((Dp, D_MODEL))
    w_in = nrm((Dp, D_MODEL, IN_COLS), D_MODEL ** -0.5)
    ssm_a_re = -0.5 * jnp.exp(nrm((Dp, SSM_GROUPS, SSM_STATE), 0.05))
    ssm_a_im = jnp.pi * jnp.arange(SSM_STATE, dtype=f32) + nrm((Dp, SSM_GROUPS, SSM_STATE), 0.01)
    ssm_log_dt = jax.random.uniform(next(it), (Dp, SSM_GROUPS), f32, math.log(1e-3), math.log(1e-1))
    ssm_b_re = nrm((Dp, SSM_GROUPS, SSM_STATE, SSM_GROUP), (2 * SSM_GROUP) ** -0.5)
    ssm_b_im = nrm((Dp, SSM_GROUPS, SSM_STATE, SSM_GROUP), (2 * SSM_GROUP) ** -0.5)
    ssm_c_re = nrm((Dp, SSM_GROUPS, SSM_GROUP, SSM_STATE), (2 * SSM_STATE) ** -0.5)
    ssm_c_im = nrm((Dp, SSM_GROUPS, SSM_GROUP, SSM_STATE), (2 * SSM_STATE) ** -0.5)
    ssm_d = nrm((Dp, SSM_WIDTH), 0.5)
    ssm_w_glu = nrm((Dp, SSM_WIDTH, SSM_WIDTH), SSM_WIDTH ** -0.5)
    ssm_b_glu = nrm((Dp, SSM_WIDTH), 0.02)
    w_ssm_out = nrm((Dp, SSM_WIDTH, D_MODEL), SSM_WIDTH ** -0.5)
    ml_conv_w = nrm((Dp, ML_CONV, ML_WIDTH), 0.5)
    ml_conv_b = nrm((Dp, ML_WIDTH), 0.02)
    nb = ML_WIDTH // ML_QKV_BLOCK
    ml_wq = nrm((Dp, nb, ML_QKV_BLOCK, ML_QKV_BLOCK), ML_QKV_BLOCK ** -0.5)
    ml_wk = nrm((Dp, nb, ML_QKV_BLOCK, ML_QKV_BLOCK), ML_QKV_BLOCK ** -0.5)
    ml_wv = nrm((Dp, nb, ML_QKV_BLOCK, ML_QKV_BLOCK), ML_QKV_BLOCK ** -0.5)
    ml_w_if = nrm((Dp, 3 * ML_WIDTH, 2 * ML_HEADS), (3 * ML_WIDTH) ** -0.5)
    ml_b_if = jnp.concatenate([nrm((Dp, ML_HEADS), 0.1),
                               3.0 + 3.0 * jax.random.uniform(next(it), (Dp, ML_HEADS), f32)], axis=-1)
    ml_norm_g = gain((Dp, ML_WIDTH))
    ml_skip = 1.0 + nrm((Dp, ML_WIDTH), 0.1)
    w_ml_out = nrm((Dp, ML_WIDTH, D_MODEL), ML_WIDTH ** -0.5)
    w_out = nrm((Dp, D_MODEL, D_MODEL), D_MODEL ** -0.5)
    norm2_g = gain((Dp, D_MODEL))
    peer_w_q = nrm((Dp, D_MODEL, PEER_HEADS * PEER_QDIM), D_MODEL ** -0.5)
    peer_sub_keys = nrm((Dp, PEER_HEADS, 2, PEER_NKEYS, PEER_HALF_2), PEER_HALF_2 ** -0.5)
    peer_u = nrm((Dp, PEER_EXPERTS, D_MODEL), D_MODEL ** -0.5)
    peer_v = nrm((Dp, PEER_EXPERTS, D_MODEL), 0.5 * PEER_HEADS ** -0.5)
    final_norm_g = gain((D_MODEL,))
    return {"x": x, "meta_tokens": meta_tokens, "norm1_g": norm1_g, "w_in": w_in,
            "ssm_a_re": ssm_a_re, "ssm_a_im": ssm_a_im, "ssm_log_dt": ssm_log_dt,
            "ssm_b_re": ssm_b_re, "ssm_b_im": ssm_b_im, "ssm_c_re": ssm_c_re, "ssm_c_im": ssm_c_im,
            "ssm_d": ssm_d, "ssm_w_glu": ssm_w_glu, "ssm_b_glu": ssm_b_glu, "w_ssm_out": w_ssm_out,
            "ml_conv_w": ml_conv_w, "ml_conv_b": ml_conv_b, "ml_wq": ml_wq, "ml_wk": ml_wk, "ml_wv": ml_wv,
            "ml_w_if": ml_w_if, "ml_b_if": ml_b_if, "ml_norm_g": ml_norm_g, "ml_skip": ml_skip,
            "w_ml_out": w_ml_out, "w_out": w_out, "norm2_g": norm2_g, "peer_w_q": peer_w_q,
            "peer_sub_keys": peer_sub_keys, "peer_u": peer_u, "peer_v": peer_v,
            "final_norm_g": final_norm_g}

def second_block(x, meta_tokens, norm1_g, w_in, ssm_a_re, ssm_a_im, ssm_log_dt, ssm_b_re, ssm_b_im,
              ssm_c_re, ssm_c_im, ssm_d, ssm_w_glu, ssm_b_glu, w_ssm_out, ml_conv_w, ml_conv_b,
              ml_wq, ml_wk, ml_wv, ml_w_if, ml_b_if, ml_norm_g, ml_skip, w_ml_out, w_out, norm2_g,
              peer_w_q, peer_sub_keys, peer_u, peer_v, final_norm_g):
    bn = x.shape[0]
    meta = jnp.broadcast_to(meta_tokens.astype(x.dtype)[None], (bn, N_META, D_MODEL))
    h = jnp.concatenate([meta, x], axis=1)
    splits = [SSM_WIDTH, SSM_WIDTH + ML_WIDTH, SSM_WIDTH + 2 * ML_WIDTH,
              SSM_WIDTH + 2 * ML_WIDTH + D_MODEL]
    for l in range(DEPTH):
        xn = rmsnorm_2(h, norm1_g[l])
        proj = xn @ w_in[l]
        u_s, x_m, z_m, g_s, g_m = jnp.split(proj, splits, axis=-1)
        y_s = s5_branch(u_s, ssm_a_re[l], ssm_a_im[l], ssm_log_dt[l], ssm_b_re[l], ssm_b_im[l],
                        ssm_c_re[l], ssm_c_im[l], ssm_d[l], ssm_w_glu[l], ssm_b_glu[l]) @ w_ssm_out[l]
        y_m = mlstm_branch(x_m, z_m, ml_conv_w[l], ml_conv_b[l], ml_wq[l], ml_wk[l], ml_wv[l],
                           ml_w_if[l], ml_b_if[l], ml_norm_g[l], ml_skip[l]) @ w_ml_out[l]
        mixed = jax.nn.sigmoid(g_s) * y_s + jax.nn.sigmoid(g_m) * y_m
        h = h + mixed @ w_out[l]
        h = h + peer_ffn_2(rmsnorm_2(h, norm2_g[l]), peer_w_q[l], peer_sub_keys[l], peer_u[l], peer_v[l])
    return rmsnorm_2(h, final_norm_g)[:, N_META:]


def setup_inputs(seed=0):
    out = dict(first_inputs(seed))
    for name, value in second_inputs(seed + 1).items():
        if name != "x":
            out[name + "_2"] = value
    return out


def reference(
    x, c, w_ada, b_ada, norm1_g, norm2_g, w_in, rel_bias, w_proj_a, w_proj_b, w_out, peer_wq,
    peer_sub_keys, peer_u, peer_v, final_g, meta_tokens_2, norm1_g_2, w_in_2, ssm_a_re_2,
    ssm_a_im_2, ssm_log_dt_2, ssm_b_re_2, ssm_b_im_2, ssm_c_re_2, ssm_c_im_2, ssm_d_2,
    ssm_w_glu_2, ssm_b_glu_2, w_ssm_out_2, ml_conv_w_2, ml_conv_b_2, ml_wq_2, ml_wk_2, ml_wv_2,
    ml_w_if_2, ml_b_if_2, ml_norm_g_2, ml_skip_2, w_ml_out_2, w_out_2, norm2_g_2, peer_w_q_2,
    peer_sub_keys_2, peer_u_2, peer_v_2, final_norm_g_2,
):
    x = first_block(
        x, c, w_ada, b_ada, norm1_g, norm2_g, w_in, rel_bias, w_proj_a, w_proj_b, w_out,
        peer_wq, peer_sub_keys, peer_u, peer_v, final_g,
    )
    return second_block(
        x, meta_tokens_2, norm1_g_2, w_in_2, ssm_a_re_2, ssm_a_im_2, ssm_log_dt_2, ssm_b_re_2,
        ssm_b_im_2, ssm_c_re_2, ssm_c_im_2, ssm_d_2, ssm_w_glu_2, ssm_b_glu_2, w_ssm_out_2,
        ml_conv_w_2, ml_conv_b_2, ml_wq_2, ml_wk_2, ml_wv_2, ml_w_if_2, ml_b_if_2, ml_norm_g_2,
        ml_skip_2, w_ml_out_2, w_out_2, norm2_g_2, peer_w_q_2, peer_sub_keys_2, peer_u_2,
        peer_v_2, final_norm_g_2,
    )


_drawn_inputs = setup_inputs


def setup_inputs(seed=0):
    import zlib

    import numpy as np

    out = dict(_drawn_inputs(seed))
    spreads = {}
    factors = {'b_ada': 3.443,
     'norm1_g': 2.896,
     'norm2_g': 2.737,
     'ssm_a_re_2': 64.0,
     'ssm_a_im_2': 39.536,
     'ssm_log_dt_2': 43.128,
     'ssm_b_re_2': 52.456,
     'ssm_b_im_2': 51.352,
     'ssm_c_re_2': 52.552,
     'ssm_c_im_2': 50.632,
     'ssm_w_glu_2': 11.217,
     'ssm_b_glu_2': 191.916,
     'ml_conv_b_2': 3.104,
     'ml_norm_g_2': 4.787,
     'norm2_g_2': 5.036,
     'final_norm_g_2': 21.984,
     'ml_skip_2': 3.291}
    for name, (base, spread) in spreads.items():
        noise = np.random.default_rng([zlib.crc32(name.encode()), seed]).standard_normal(out[name].shape)
        drawn = base * np.exp(spread * noise) if base else spread * noise
        out[name] = __import__('jax').numpy.asarray(drawn.astype(out[name].dtype))
    for name, factor in factors.items():
        out[name] = (out[name] * factor).astype(out[name].dtype)
    return out
```

```python
import math
from contextlib import ExitStack

import numpy as np

import concourse.bass as bass
from concourse import mybir

F32 = mybir.dt.float32
I32 = mybir.dt.int32
U32 = mybir.dt.uint32
ALU = mybir.AluOpType
ACT = mybir.ActivationFunctionType
AX = mybir.AxisListType

P = 128
D = 1024
KD = D // P
TOK = 256
TT = TOK // P
META = 16
TALL = TOK + META
HEADS = 8
DH = 64
PAIRS = HEADS // 2
IDX_SCALE = 64 ** -0.5 * 8 ** -0.5
TOPK = 64
BUCKETS = 32
PH = 8
PK = 16
NKEYS = 128
EPS = 1e-6
S5G, S5C, S5N = 32, 16, 64
MH, MDH = 4, 256
SLOTS = 4
CHUNK = 2048
BANKS = 8
CREDIT = 8
NEG = -1.0e38
TAKEN = -3.0e38
BIG = 1.0e30

GRID = []
_at = 0
for _a, _b, _w in ((0, 1, 16), (1, 2, 8), (2, 4, 5), (4, 8, 3), (8, 16, 1)):
    GRID.append((_a, _b, _w, _at))
    _at += (_b - _a) * _w
NCAND = _at

VEC = {}
_at = 0
for _n, _c in (("c", 8), ("b_ada", 48), ("norm1_g", 8), ("norm2_g", 8), ("final_g", 8), ("norm1_g_2", 8),
               ("ssm_d_2", 4), ("ssm_b_glu_2", 4), ("ml_conv_w_2", 32), ("ml_conv_b_2", 8), ("ml_norm_g_2", 8),
               ("ml_skip_2", 8), ("norm2_g_2", 8), ("final_norm_g_2", 8)):
    VEC[_n] = slice(_at, _at + _c)
    _at += _c
NVEC = _at

CHUNKS = {}
_at = 0
for _n, _c in (("ada", 24), ("in1", 18), ("v1", 4), ("ki", 1), ("projab", 4), ("out1", 4), ("wq1", 8), ("keys1", 1),
               ("uv1", 128), ("in2", 18), ("glu", 1), ("ssmout", 2), ("mlout", 4), ("out2", 4),
               ("wq2", 8), ("keys2", 1), ("uv2", 128)):
    CHUNKS[_n] = (_at, _at + _c)
    _at += _c
NCHUNKS = _at


def experts_of(c):
    for layer in "12":
        if CHUNKS["uv" + layer][0] <= c < CHUNKS["uv" + layer][1]:
            return layer, c - CHUNKS["uv" + layer][0]
    return None


DENSE_AT = {}
LOADED = []
for _c in range(NCHUNKS):
    if experts_of(_c) is None:
        DENSE_AT[_c] = len(DENSE_AT)
    LOADED.append((LOADED[_c - SLOTS] if _c >= SLOTS else 0) + (32 if experts_of(_c) else 16))
NDENSE = len(DENSE_AT)

C_ID, C_IOTA, C_LOW, C_STRICT, C_UP, C_BD = (slice(i * P, (i + 1) * P) for i in range(6))
C_GRP = slice(6 * P, 6 * P + 8)
NCONST = 6 * P + 8


class Signal:

    def __init__(self, sem):
        self.sem, self.base = sem, CREDIT

    def at(self, n):
        return n + self.base

    def advance(self, n):
        self.base += n


class Chain:

    def __init__(self, eng, steps):
        self.eng, self.steps = eng, steps

    def __call__(self, ins):
        ins.then_inc(self.steps.sem, 1)
        self.steps.base += 1

    def wait(self):
        self.eng.wait_ge(self.steps.sem, self.steps.base)

    def then(self, ins):
        self(ins)
        self.wait()


class K:
    pass


def rounds(eng, n, per, body):
    full = n // per
    if full >= 2:
        with eng.Fori(0, full) as it:
            for j in range(per):
                body(it * per, it, j)
        done = full
    else:
        done = 0
    for r in range(done, (n + per - 1) // per):
        for j in range(min(per, n - r * per)):
            body(r * per, r, j)


def load_chunk(k, sp, c, more=0):
    slot, loaded = c % SLOTS, k.w_loaded[c % SLOTS]
    experts = experts_of(c)
    if experts is None:
        sp.dma_start(k.ring[:, slot, :], k.args["dense"][bass.ds(more + DENSE_AT[c], 1), :, :]
                     .rearrange("a p n -> (a p) n")).then_inc(loaded, 16)
        return
    layer, e = experts
    for half, name in enumerate(("u", "v")):
        sp.dma_start(k.ring[:, slot, half * D:(half + 1) * D], k.args[name + layer][bass.ds(more + e, 1), :, :]
                     .rearrange("a p n -> (a p) n")).then_inc(loaded, 16)


def refill(k, sp, n, used, per):
    a = k.chunk
    n = min(n, NCHUNKS - SLOTS - a)
    c = 0
    while c < n:
        kind = lambda i: (experts_of(a + i + SLOTS) or (None,))[0]
        run = 1
        while c + run < n and kind(c + run) == kind(c):
            run += 1
        full = run // SLOTS if not isinstance(per, list) else 0
        if full >= 2:
            with sp.Fori(0, full) as it:
                for j in range(c, c + SLOTS):
                    sp.wait_ge(used.sem, it * (SLOTS * per) + used.at((j + 1) * per))
                    load_chunk(k, sp, a + j + SLOTS, it * SLOTS)
            c += full * SLOTS
        else:
            sp.wait_ge(used.sem, used.at(per[c] if isinstance(per, list) else (c + 1) * per))
            load_chunk(k, sp, a + c + SLOTS)
            c += 1


def chunk_wait(k, eng, it, jj):
    c = k.chunk + jj
    eng.wait_ge(k.w_loaded[c % SLOTS], it * (32 if experts_of(c) else 16) + LOADED[c])
    return k.ring[:, c % SLOTS, :]


def linear_t(k, ntiles, nk, rhs, cols, evac, who="alt"):
    nc = k.nc
    tpc = CHUNK // (nk * P)
    per = SLOTS * tpc if SLOTS * tpc <= BANKS else BANKS
    nchunks = ntiles // tpc
    emptied = {"act": k.act_emptied, "dve": k.dve_emptied}

    def mine(j):
        return who if who != "alt" else ("act", "dve")[j % 2]

    with nc.Block() as block:
        @block.sync
        def _(sp):
            refill(k, sp, nchunks, k.tile_ready, tpc)

        @block.tensor
        def _(pe):
            def tile(first, it, j):
                if isinstance(first, int):
                    before = (first + j) // 2 if who == "alt" else first + j
                    c = (first + j) // tpc
                    rit, jj = c // SLOTS, c % SLOTS
                else:
                    before = it * (per // 2) + j // 2 if who == "alt" else first + j
                    rit, jj = it, j // tpc
                if j % tpc == 0:
                    slot = chunk_wait(k, pe, rit, jj)
                else:
                    slot = k.ring[:, (k.chunk + jj) % SLOTS, :]
                w = slot.rearrange("p (k n) -> p k n", k=nk)
                ahead = BANKS // 2 if who == "alt" else BANKS
                pe.wait_ge(emptied[mine(j)].sem, before + (emptied[mine(j)].base - ahead + 1))
                out = k.bank[j % BANKS][:, 0:cols]
                n0 = (j % tpc) * P
                for kk in range(nk):
                    ins = nc.tensor.matmul(out, w[:, kk, n0:n0 + P], rhs(kk), start=kk == 0, stop=kk == nk - 1)
                ins.then_inc(k.tile_ready.sem, 1)
            rounds(pe, ntiles, per, tile)

        def emptying(eng, name):
            def tile(first, it, j):
                if mine(j) != name:
                    return
                eng.wait_ge(k.tile_ready.sem, first + (k.tile_ready.base + j + 1))
                evac(name, first + j, k.bank[j % BANKS][:, 0:cols]).then_inc(emptied[name].sem, 1)
            rounds(eng, ntiles, per, tile)

        if who != "dve":
            @block.scalar
            def _(act):
                emptying(act, "act")

        if who != "act":
            @block.vector
            def _(dve):
                emptying(dve, "dve")

    k.chunk += nchunks
    k.tile_ready.advance(ntiles)
    if who == "alt":
        k.act_emptied.advance(ntiles // 2)
        k.dve_emptied.advance(ntiles // 2)
    else:
        emptied[who].advance(ntiles)


def copy_to(k, dst):
    def evac(name, i, ps):
        out = dst[:, bass.ds(i, 1), :].rearrange("p a n -> p (a n)")
        if name == "act":
            return k.nc.scalar.activation(out, ps, ACT.Copy)
        return k.nc.vector.tensor_copy(out, ps)
    return evac


def rmsnorm_t(k, src, cols, dst, gain, shift):
    nc = k.nc
    with ExitStack() as ctx:
        sq = ctx.enter_context(nc.sbuf_tensor(k.name("sq"), [P, KD, TALL], F32))
        rs = ctx.enter_context(nc.sbuf_tensor(k.name("rs"), [P, 2, TALL], F32))
        with nc.Block() as block:
            @block.vector
            def _(dve):
                ch = Chain(dve, k.dve_step)
                nc.vector.tensor_tensor(sq[:, :, 0:cols], src, src, ALU.mult).then_inc(k.sq_ready.sem, 1)
                dve.wait_ge(k.tile_ready.sem, k.tile_ready.at(1))
                ch.then(nc.vector.tensor_scalar(rs[:, 0, 0:cols], k.bank[0][:, 0:cols], 1.0 / D, EPS, ALU.mult, ALU.add))
                nc.vector.reciprocal(rs[:, 1, 0:cols], rs[:, 0, 0:cols]).then_inc(k.recip_ready.sem, 1)
                dve.wait_ge(k.act_emptied.sem, k.act_emptied.at(1))
                nc.vector.tensor_tensor(sq[:, :, 0:cols], src, rs[:, 0:1, 0:cols].broadcast_to([P, KD, cols]),
                                        ALU.mult).then_inc(k.sq_ready.sem, 1)

            @block.tensor
            def _(pe):
                pe.wait_ge(k.sq_ready.sem, k.sq_ready.at(1))
                for kk in range(KD):
                    ins = nc.tensor.matmul(k.bank[0][:, 0:cols], k.ones[:, :], sq[:, kk, 0:cols],
                                           start=kk == 0, stop=kk == KD - 1)
                ins.then_inc(k.tile_ready.sem, 1)

            @block.scalar
            def _(act):
                act.wait_ge(k.recip_ready.sem, k.recip_ready.at(1))
                nc.scalar.activation(rs[:, 0, 0:cols], rs[:, 1, 0:cols], ACT.Sqrt).then_inc(k.act_emptied.sem, 1)
                act.wait_ge(k.sq_ready.sem, k.sq_ready.at(2))
                for kk in range(KD):
                    nc.scalar.activation(dst[:, kk, :], sq[:, kk, 0:cols], ACT.Identity,
                                         scale=gain[:, kk:kk + 1],
                                         bias=0.0 if shift is None else shift[:, kk:kk + 1])
    k.sq_ready.advance(2)
    k.tile_ready.advance(1)
    k.recip_ready.advance(1)
    k.act_emptied.advance(1)


def modulation(k):
    nc = k.nc
    with ExitStack() as ctx:
        cond = ctx.enter_context(nc.sbuf_tensor("cond", [P, KD], F32))
        ntiles = 6 * KD
        with nc.Block() as block:
            @block.sync
            def _(sp):
                refill(k, sp, ntiles // 2, k.w_used, 1)

            @block.scalar
            def _(act):
                nc.scalar.activation(cond[:, :], k.vec("c"), ACT.Silu).then_inc(k.recip_ready.sem, 1)

            @block.tensor
            def _(pe):
                pe.wait_ge(k.recip_ready.sem, k.recip_ready.at(1))

                def tile(first, it, j):
                    slot = chunk_wait(k, pe, it, j // 2) if j % 2 == 0 else k.ring[:, (k.chunk + j // 2) % SLOTS, :]
                    w = slot.rearrange("p (k n) -> p k n", k=KD)
                    for kk in range(KD):
                        ins = nc.tensor.matmul(k.bank[0][:, bass.ds(first + j, 1)], w[:, kk, (j % 2) * P:(j % 2 + 1) * P],
                                               cond[:, kk:kk + 1], start=kk == 0, stop=kk == KD - 1)
                    if j % 2:
                        ins.then_inc(k.w_used.sem, 1)
                rounds(pe, ntiles, 2 * SLOTS, tile)

            @block.vector
            def _(dve):
                ch = Chain(dve, k.dve_step)
                dve.wait_ge(k.w_used.sem, k.w_used.at(ntiles // 2))
                ch.then(nc.vector.tensor_tensor(k.mod[:, :], k.bank[0][:, 0:ntiles], k.vec("b_ada"), ALU.add))
                for n, g in ((0, "norm1_g"), (1, "norm2_g")):
                    nc.vector.scalar_tensor_tensor(k.gain[:, n, :], k.mod[:, (3 * n + 1) * KD:(3 * n + 2) * KD], 1.0,
                                                   k.vec(g), ALU.add, ALU.mult)
    k.recip_ready.advance(1)
    k.w_used.advance(ntiles // 2)
    k.chunk += ntiles // 2


def block1_projections(k, pt, v, kit, wi):
    nc = k.nc
    linear_t(k, 36, KD, lambda kk: k.h[:, kk, 0:TOK], TOK, copy_to(k, pt))
    with nc.Block() as block:
        @block.sync
        def _(sp):
            refill(k, sp, 5, k.tile_ready, 2)

        @block.tensor
        def _(pe):
            for c in range(4):
                w = chunk_wait(k, pe, 0, c).rearrange("p (k n) -> p k n", k=KD)
                for tt in range(TT):
                    for kk in range(KD):
                        ins = nc.tensor.matmul(k.bank[2 * c + tt][:, 0:256], k.h[:, kk, tt * P:(tt + 1) * P], w[:, kk, :],
                                               start=kk == 0, stop=kk == KD - 1)
                    ins.then_inc(k.tile_ready.sem, 1)
            w = chunk_wait(k, pe, 0, 4).rearrange("p (k n) -> p k n", k=KD)
            pe.wait_ge(k.act_emptied.sem, k.act_emptied.at(1))
            for kk in range(KD):
                ins = nc.tensor.matmul(k.bank[0][:, 0:TOK], w[:, kk, 0:P], k.h[:, kk, 0:TOK],
                                       start=kk == 0, stop=kk == KD - 1)
            ins.then_inc(k.tile_ready.sem, 1)
            pe.wait_ge(k.dve_emptied.sem, k.dve_emptied.at(1))
            for tt in range(TT):
                for kk in range(KD):
                    ins = nc.tensor.matmul(k.bank[1][:, tt * 8:tt * 8 + 8], k.h[:, kk, tt * P:(tt + 1) * P],
                                           w[:, kk, P:P + 8], start=kk == 0, stop=kk == KD - 1)
            ins.then_inc(k.tile_ready.sem, 1)

        @block.scalar
        def _(act):
            for c in range(4):
                act.wait_ge(k.tile_ready.sem, k.tile_ready.at(2 * c + 1))
                nc.scalar.activation(v[:, 0, c * 256:(c + 1) * 256], k.bank[2 * c][:, 0:256], ACT.Copy)\
                    .then_inc(k.act_emptied.sem, 1)
            act.wait_ge(k.tile_ready.sem, k.tile_ready.at(9))
            nc.scalar.activation(kit[:, :], k.bank[0][:, 0:TOK], ACT.Copy)

        @block.vector
        def _(dve):
            for c in range(4):
                dve.wait_ge(k.tile_ready.sem, k.tile_ready.at(2 * c + 2))
                nc.vector.tensor_copy(v[:, 1, c * 256:(c + 1) * 256], k.bank[2 * c + 1][:, 0:256])\
                    .then_inc(k.dve_emptied.sem, 1)
            dve.wait_ge(k.tile_ready.sem, k.tile_ready.at(10))
            nc.vector.tensor_scalar(wi[:, :], k.bank[1][:, 0:16], IDX_SCALE, None, ALU.mult)
    k.tile_ready.advance(10)
    k.act_emptied.advance(4)
    k.dve_emptied.advance(4)
    k.chunk += 5


def position_bias(k, bias):
    nc = k.nc
    width = 3 * P
    with ExitStack() as ctx:
        row = ctx.enter_context(nc.sbuf_tensor("bias_row", [P, HEADS, width], F32))
        rel = ctx.enter_context(nc.sbuf_tensor("rel_spread", [BUCKETS, HEADS, P], F32))
        with nc.Block() as block:
            @block.tensor
            def _(pe):
                pe.wait_ge(k.dve_emptied.sem, k.dve_emptied.at(1))
                for h in range(HEADS):
                    nc.tensor.matmul(k.bank[h][:, 0:width], rel[:, h, :], k.onehot[:, :],
                                     start=True, stop=True).then_inc(k.tile_ready.sem, 1)

            @block.vector
            def _(dve):
                nc.vector.tensor_copy(rel[:, :, :], k.rel[:, :].unsqueeze(2).broadcast_to([BUCKETS, HEADS, P]))\
                    .then_inc(k.dve_emptied.sem, 1)
                for h in range(HEADS):
                    dve.wait_ge(k.tile_ready.sem, k.tile_ready.at(h + 1))
                    nc.vector.tensor_copy(row[:, h, :], k.bank[h][:, 0:width]).then_inc(k.dve_emptied.sem, 1)

            @block.gpsimd
            def _(pool):
                pool.wait_ge(k.dve_emptied.sem, k.dve_emptied.at(HEADS + 1))
                pool.dma_start(k.bias_dram, row[:, :, :]).then_inc(k.bias_dma, 16)
                pool.wait_ge(k.bias_dma, 16)
                src = bass.AP(k.bias_dram.tensor, P - 1, [[HEADS * width - 1, P], [width, HEADS], [1, 2 * P]])
                pool.dma_start(bias[:, :, :], src).then_inc(k.bias_dma, 16)
                pool.wait_ge(k.bias_dma, 32)
    k.tile_ready.advance(HEADS)
    k.dve_emptied.advance(HEADS + 1)


def index_selection(k, pt, kit, wi, bias0, bias1):
    nc = k.nc
    with ExitStack() as ctx:
        relu = ctx.enter_context(nc.sbuf_tensor("relu", [P, 4, TOK], F32))
        score = ctx.enter_context(nc.sbuf_tensor("score", [P, TT, TOK], F32))
        top = ctx.enter_context(nc.sbuf_tensor("top", [P, TT, 8], F32))
        mask = ctx.enter_context(nc.sbuf_tensor("negmask", [P, P], F32))
        items = [(tt, h) for tt in range(TT) for h in range(HEADS)]
        with nc.Block() as block:
            @block.tensor
            def _(pe):
                for n, (tt, h) in enumerate(items):
                    s, r = P * (tt + 1), slice(64 * (h % 2), 64 * (h % 2) + 64)
                    pe.wait_ge(k.act_emptied.sem, k.act_emptied.at(n - 3))
                    nc.tensor.matmul(k.bank[n % 4][:, 0:s], pt[r, 8 + h // 2, tt * P:(tt + 1) * P], kit[r, 0:s],
                                     start=True, stop=True).then_inc(k.tile_ready.sem, 1)

            @block.scalar
            def _(act):
                for n, (tt, h) in enumerate(items):
                    s = P * (tt + 1)
                    act.wait_ge(k.tile_ready.sem, k.tile_ready.at(n + 1))
                    act.wait_ge(k.dve_emptied.sem, k.dve_emptied.at(n - 3))
                    nc.scalar.activation(relu[:, n % 4, 0:s], k.bank[n % 4][:, 0:s], ACT.Relu)\
                        .then_inc(k.act_emptied.sem, 1)

            @block.vector
            def _(dve):
                ch = Chain(dve, k.dve_step)
                ch.then(nc.vector.tensor_scalar(mask[:, :], k.const[:, C_LOW], -NEG, NEG, ALU.mult, ALU.add))
                for n, (tt, h) in enumerate(items):
                    s = P * (tt + 1)
                    dve.wait_ge(k.act_emptied.sem, k.act_emptied.at(n + 1))
                    w = wi[:, tt * 8 + h:tt * 8 + h + 1]
                    if h == 0:
                        ins = nc.vector.tensor_scalar(score[:, tt, 0:s], relu[:, n % 4, 0:s], w, None, ALU.mult)
                    else:
                        ins = nc.vector.scalar_tensor_tensor(score[:, tt, 0:s], relu[:, n % 4, 0:s], w,
                                                             score[:, tt, 0:s], ALU.mult, ALU.add)
                    ins.then_inc(k.dve_emptied.sem, 1)
                    dve.wait_ge(k.dve_emptied.sem, k.dve_emptied.at(n + 1))
                for tt in range(TT):
                    diag = score[:, tt, tt * P:(tt + 1) * P]
                    ch.then(nc.vector.tensor_tensor(diag, diag, k.const[:, C_LOW], ALU.mult))
                    ch.then(nc.vector.tensor_tensor(diag, diag, mask[:, :], ALU.add))
                for _ in range(TOPK // 8):
                    for tt in range(TT):
                        ch(nc.vector.max(top[:, tt, :], score[:, tt, 0:P * (tt + 1)]))
                    ch.wait()
                    for tt in range(TT):
                        ch(nc.vector.match_replace(score[:, tt, 0:P * (tt + 1)], top[:, tt, :],
                                                   score[:, tt, 0:P * (tt + 1)], TAKEN))
                    ch.wait()
                for tt in range(TT):
                    s = P * (tt + 1)
                    sc, diag = score[:, tt, 0:s], score[:, tt, tt * P:s]
                    ch.then(nc.vector.tensor_scalar(sc, sc, 2 * NEG, None, ALU.is_lt))
                    ch.then(nc.vector.tensor_tensor(diag, diag, k.const[:, C_LOW], ALU.mult))
                    ch.then(nc.vector.tensor_scalar(sc, sc, BIG, -BIG, ALU.mult, ALU.add))
                s0 = score[:, 0:1, 0:P].broadcast_to([P, HEADS, P])
                ch.then(nc.vector.tensor_tensor(bias0[:, :, :], bias1[:, :, P:2 * P], s0, ALU.add))
                s1 = score[:, 1:2, :].broadcast_to([P, HEADS, 2 * P])
                nc.vector.tensor_tensor(bias1[:, :, :], bias1[:, :, :], s1, ALU.add)
    k.tile_ready.advance(16)
    k.act_emptied.advance(16)
    k.dve_emptied.advance(16)


def attentions(k, pt, v, bias0, bias1, yt):
    nc = k.nc
    items = [(kind, tt, h) for kind in (0, 1) for tt in range(TT) for h in range(HEADS)]
    n_items = len(items)
    B2 = 2
    with ExitStack() as ctx:
        lg = ctx.enter_context(nc.sbuf_tensor("logits", [P, B2, TOK], F32))
        ex = ctx.enter_context(nc.sbuf_tensor("expd", [P, B2, TOK], F32))
        pr = ctx.enter_context(nc.sbuf_tensor("probs", [P, B2, TOK], F32))
        prt = ctx.enter_context(nc.sbuf_tensor("probs_t", [P, B2, TT, P], F32))
        betas = ctx.enter_context(nc.sbuf_tensor("beta", [P, B2, TOK], F32))
        oms = ctx.enter_context(nc.sbuf_tensor("one_minus", [P, B2, TOK], F32))
        prod = [ctx.enter_context(nc.sbuf_tensor(f"product{tt}", [P, P * (tt + 1) + 1], F32)) for tt in range(TT)]
        small = ctx.enter_context(nc.sbuf_tensor("small", [P, B2, 4], F32))
        inv = ctx.enter_context(nc.sbuf_tensor("not_strict", [P, P], F32))
        qk, mid, prob = k.qk_ready, k.weights_ready, k.probs_ready
        with nc.Block() as block:
            @block.tensor
            def _(pe):
                def scores(n):
                    kind, tt, h = items[n]
                    s, r = P * (tt + 1), slice(64 * (h % 2), 64 * (h % 2) + 64)
                    q, kk = (0, 4) if kind == 0 else (12, 16)
                    pe.wait_ge(prob.sem, prob.at(n - 1))
                    nc.tensor.matmul(k.bank[n % 2][:, 0:s], pt[r, q + h // 2, tt * P:(tt + 1) * P],
                                     pt[r, kk + h // 2, 0:s], start=True, stop=True).then_inc(qk.sem, 1)

                def values(n):
                    kind, tt, h = items[n]
                    pe.wait_ge(k.act_emptied.sem, k.act_emptied.at(n + 1))
                    pe.wait_ge(k.dve_emptied.sem, k.dve_emptied.at(n - 1))
                    pair = h // 2
                    for j in range(tt + 1):
                        ins = nc.tensor.matmul(k.bank[4 + n % 2][:, 0:P],
                                               v[:, j, kind * 512 + pair * P:kind * 512 + (pair + 1) * P],
                                               prt[:, n % 2, j, :], start=j == 0, stop=j == tt)
                    ins.then_inc(k.tile_ready.sem, 1)

                scores(0)
                for n, (kind, tt, h) in enumerate(items):
                    if n + 1 < n_items:
                        scores(n + 1)
                    pe.wait_ge(prob.sem, prob.at(n + 1))
                    pe.wait_ge(k.act_emptied.sem, k.act_emptied.at(n - 1))
                    for j in range(tt + 1):
                        ins = nc.tensor.transpose(k.bank[2 + n % 2][:, j * P:(j + 1) * P],
                                                  pr[:, n % 2, j * P:(j + 1) * P], k.const[:, C_ID])
                    ins.then_inc(k.trans_ready.sem, 1)
                    if n:
                        values(n - 1)
                values(n_items - 1)

            @block.scalar
            def _(act):
                def copy(n):
                    kind, tt, h = items[n]
                    act.wait_ge(k.trans_ready.sem, k.trans_ready.at(n + 1))
                    act.wait_ge(k.tile_ready.sem, k.tile_ready.at(n - 1))
                    nc.scalar.activation(prt[:, n % 2, 0:tt + 1, :].rearrange("p a b -> p (a b)"),
                                         k.bank[2 + n % 2][:, 0:(tt + 1) * P], ACT.Copy)\
                        .then_inc(k.act_emptied.sem, 1)

                for n, (kind, tt, h) in enumerate(items):
                    s, b = P * (tt + 1), n % 2
                    beta, om = betas[:, b, :], oms[:, b, :]
                    if kind == 0:
                        act.wait_ge(k.sq_ready.sem, k.sq_ready.at(n + 1))
                        nc.scalar.activation(ex[:, b, 0:s], lg[:, b, 0:s], ACT.Exp, bias=small[:, b, 0:1],
                                             accum_out=small[:, b, 1:2]).then_inc(mid.sem, 1)
                    else:
                        act.wait_ge(qk.sem, qk.at(n + 1))
                        act.wait_ge(prob.sem, prob.at(n - 1))
                        nc.scalar.activation(beta[:, 0:s], k.bank[b][:, 0:s], ACT.Sigmoid, scale=DH ** -0.5)
                        nc.scalar.activation(om[:, 0:s], k.bank[b][:, 0:s], ACT.Sigmoid, scale=-DH ** -0.5)\
                            .then_inc(mid.sem, 1)
                    if n:
                        copy(n - 1)
                copy(n_items - 1)

            @block.vector
            def _(dve):
                ch = Chain(dve, k.dve_step)
                ch(nc.vector.memset(prod[0][:, P:P + 1], 1.0))
                ch(nc.vector.memset(prod[1][:, 2 * P:2 * P + 1], 1.0))
                ch.then(nc.vector.tensor_scalar(inv[:, :], k.const[:, C_STRICT], -1.0, 1.0, ALU.mult, ALU.add))

                def output(n):
                    kind, tt, h = items[n]
                    r = slice(64 * (h % 2), 64 * (h % 2) + 64)
                    dve.wait_ge(k.tile_ready.sem, k.tile_ready.at(n + 1))
                    nc.vector.tensor_copy(yt[r, kind * 4 + h // 2, tt * P:(tt + 1) * P], k.bank[4 + n % 2][r, 0:P])\
                        .then_inc(k.dve_emptied.sem, 1)

                for n, (kind, tt, h) in enumerate(items):
                    s, b = P * (tt + 1), n % 2
                    beta, om = betas[:, b, :], oms[:, b, :]
                    bias = (bias0, bias1)[tt]
                    if kind == 0:
                        dve.wait_ge(qk.sem, qk.at(n + 1))
                        ch.then(nc.vector.scalar_tensor_tensor(lg[:, b, 0:s], k.bank[b][:, 0:s], DH ** -0.5,
                                                               bias[:, h, 0:s], ALU.mult, ALU.add))
                        nc.vector.tensor_reduce(small[:, b, 0:1], lg[:, b, 0:s], AX.X, ALU.max, negate=True)\
                            .then_inc(k.sq_ready.sem, 1)
                        dve.wait_ge(mid.sem, mid.at(n + 1))
                        ch.then(nc.vector.reciprocal(small[:, b, 2:3], small[:, b, 1:2]))
                        dve.wait_ge(k.trans_ready.sem, k.trans_ready.at(n - 1))
                        nc.vector.tensor_scalar(pr[:, b, 0:s], ex[:, b, 0:s], small[:, b, 2:3], None, ALU.mult)\
                            .then_inc(prob.sem, 1)
                    else:
                        dve.wait_ge(mid.sem, mid.at(n + 1))
                        diag = slice(tt * P, s)
                        ch(nc.vector.tensor_tensor(beta[:, diag], beta[:, diag], k.const[:, C_STRICT], ALU.mult))
                        ch.then(nc.vector.tensor_tensor(om[:, diag], om[:, diag], k.const[:, C_STRICT], ALU.mult))
                        ch.then(nc.vector.tensor_tensor(om[:, diag], om[:, diag], inv[:, :], ALU.add))
                        ch.then(nc.vector.tensor_tensor_scan(prod[tt][:, 0:s][:, ::-1], om[:, 0:s][:, ::-1],
                                                             om[:, 0:s][:, ::-1], 1.0, ALU.mult, ALU.bypass))
                        dve.wait_ge(k.trans_ready.sem, k.trans_ready.at(n - 1))
                        nc.vector.tensor_tensor(pr[:, b, 0:s], beta[:, 0:s], prod[tt][:, 1:s + 1], ALU.mult)\
                            .then_inc(prob.sem, 1)
                    if n:
                        output(n - 1)
                output(n_items - 1)
    for sig in (qk, mid, prob, k.trans_ready, k.tile_ready, k.act_emptied, k.dve_emptied):
        sig.advance(n_items)
    k.sq_ready.advance(n_items // 2)


def merge1(k, pt, yt, merged):
    nc = k.nc
    with ExitStack() as ctx:
        part = ctx.enter_context(nc.sbuf_tensor("part", [P, 4, TOK], F32))
        with nc.Block() as block:
            @block.sync
            def _(sp):
                refill(k, sp, 4, k.tile_ready, [4, 4, 8, 8])

            @block.tensor
            def _(pe):
                for i in range(KD):
                    for side in range(2):
                        c = 2 * (i // 4) + side
                        slot = chunk_wait(k, pe, 0, c) if i % 4 == 0 else k.ring[:, (k.chunk + c) % SLOTS, :]
                        w = slot.rearrange("p (k n) -> p k n", k=4)
                        if side == 0:
                            pe.wait_ge(k.dve_emptied.sem, k.dve_emptied.at(i - 3))
                        for kk in range(4):
                            ins = nc.tensor.matmul(k.bank[2 * (i % 4) + side][:, 0:TOK], w[:, kk, (i % 4) * P:(i % 4 + 1) * P],
                                                   yt[:, side * 4 + kk, :], start=kk == 0, stop=kk == 3)
                    ins.then_inc(k.tile_ready.sem, 1)

            @block.scalar
            def _(act):
                for side in range(2):
                    g = pt[:, 20 + 8 * side:28 + 8 * side, :]
                    nc.scalar.activation(g, g, ACT.Sigmoid).then_inc(k.recip_ready.sem, 1)

            @block.vector
            def _(dve):
                ch = Chain(dve, k.dve_step)
                dve.wait_ge(k.recip_ready.sem, k.recip_ready.at(2))
                for i in range(KD):
                    dve.wait_ge(k.tile_ready.sem, k.tile_ready.at(i + 1))
                    ch(nc.vector.tensor_tensor(part[:, i % 4, :], pt[:, 20 + i, :], k.bank[2 * (i % 4)][:, 0:TOK], ALU.mult))
                    ins = nc.vector.tensor_tensor(merged[:, i, :], pt[:, 28 + i, :], k.bank[2 * (i % 4) + 1][:, 0:TOK], ALU.mult)
                    ins.then_inc(k.dve_emptied.sem, 1)
                    dve.wait_ge(k.dve_emptied.sem, k.dve_emptied.at(i + 1))
                    ch.then(nc.vector.tensor_tensor(merged[:, i, :], merged[:, i, :], part[:, i % 4, :], ALU.add))
    k.tile_ready.advance(KD)
    k.dve_emptied.advance(KD)
    k.recip_ready.advance(2)
    k.chunk += 4


def add_residual(k, gate):
    def evac(name, i, ps):
        x = k.x[:, bass.ds(i, 1), META:].rearrange("p a n -> p (a n)")
        if gate is None:
            return k.nc.vector.tensor_tensor(x, ps, x, ALU.add)
        return k.nc.vector.scalar_tensor_tensor(x, ps, gate[:, bass.ds(i, 1)], x, ALU.mult, ALU.add)
    return evac


def peer_select(k):
    nc = k.nc
    with ExitStack() as ctx:
        sb = lambda n, s, d=F32: ctx.enter_context(nc.sbuf_tensor(k.name(n), s, d))
        qt = sb("queries_t", [P, 2 * PH, TOK])
        s = sb("key_scores", [P, TT, 2 * PH, NKEYS])
        linear_t(k, 2 * PH, KD, lambda kk: k.h[:, kk, 0:TOK], TOK, copy_to(k, qt))
        with nc.Block() as block:
            @block.sync
            def _(sp):
                refill(k, sp, 1, k.tile_ready, 8)

            @block.tensor
            def _(pe):
                keys = chunk_wait(k, pe, 0, 0).rearrange("p (c n) -> p c n", n=NKEYS)
                for tt in range(TT):
                    for q in range(4):
                        for c in range(4 * q, 4 * q + 4):
                            ins = nc.tensor.matmul(k.bank[4 * tt + q][:, (c % 4) * P:(c % 4 + 1) * P],
                                                   qt[:, c, tt * P:(tt + 1) * P], keys[:, c, :], start=True, stop=True)
                        ins.then_inc(k.tile_ready.sem, 1)

            @block.scalar
            def _(act):
                for n in range(8):
                    act.wait_ge(k.tile_ready.sem, k.tile_ready.at(n + 1))
                    nc.scalar.activation(s[:, n // 4, 4 * (n % 4):4 * (n % 4) + 4, :].rearrange("p a n -> p (a n)"),
                                         k.bank[n][:, :], ACT.Copy)
        k.tile_ready.advance(8)
        k.chunk += 1

        NC2 = 2 * PH
        best = sb("best", [P, NC2, PK])
        best_i = sb("best_index", [P, NC2, PK], U32)
        best_f = sb("best_index_f", [P, NC2, PK])
        cand = sb("cand", [P, PH, NCAND])
        code = sb("cand_code", [P, PH, NCAND])
        left = sb("left", [P, PH, NCAND])
        top = sb("top_sum", [P, PH, PK])
        pos = sb("top_pos", [P, PH, PK], U32)
        posf = sb("top_pos_f", [P, PH, PK])
        hot = sb("hot", [P, PH, PK, NCAND])
        tot = sb("total", [P, 2, PH])
        picked = sb("picked", [P, TT, 3, P])
        whole = sb("picked_int", [P, 2, P], I32)
        with nc.Block() as block:
            @block.vector
            def _(dve):
                ch = Chain(dve, k.dve_step)
                for tt in range(TT):
                    for c in range(NC2):
                        ch(nc.vector.max(best[:, c, 0:8], s[:, tt, c, :]))
                    ch.wait()
                    for c in range(NC2):
                        ch(nc.vector.max_index(best_i[:, c, 0:8], best[:, c, 0:8], s[:, tt, c, :]))
                    for c in range(NC2):
                        ch(nc.vector.match_replace(s[:, tt, c, :], best[:, c, 0:8], s[:, tt, c, :], TAKEN))
                    ch.wait()
                    for c in range(NC2):
                        ch(nc.vector.max(best[:, c, 8:16], s[:, tt, c, :]))
                    ch.wait()
                    for c in range(NC2):
                        ch(nc.vector.max_index(best_i[:, c, 8:16], best[:, c, 8:16], s[:, tt, c, :]))
                    ch.wait()
                    ch.then(nc.vector.tensor_copy(best_f[:, :, :], best_i[:, :, :]))
                    bv = best[:, :, :].rearrange("p (h c) n -> p h c n", c=2)
                    bf = best_f[:, :, :].rearrange("p (h c) n -> p h c n", c=2)
                    ch.then(nc.vector.tensor_scalar(bf[:, :, 0, :], bf[:, :, 0, :], float(NKEYS), None, ALU.mult))
                    for src, dst in ((bv, cand), (bf, code)):
                        for i0, i1, w, at in GRID:
                            shape = [P, PH, i1 - i0, w]
                            ch(nc.vector.tensor_tensor(
                                dst[:, :, at:at + (i1 - i0) * w].rearrange("p h (i j) -> p h i j", j=w),
                                src[:, :, 0, i0:i1].unsqueeze(3).broadcast_to(shape),
                                src[:, :, 1, 0:w].unsqueeze(2).broadcast_to(shape), ALU.add))
                    ch.wait()
                    for h in range(PH):
                        ch(nc.vector.max(top[:, h, 0:8], cand[:, h, :]))
                    ch.wait()
                    for h in range(PH):
                        ch(nc.vector.max_index(pos[:, h, 0:8], top[:, h, 0:8], cand[:, h, :]))
                        ch(nc.vector.match_replace(left[:, h, :], top[:, h, 0:8], cand[:, h, :], TAKEN))
                    ch.wait()
                    for h in range(PH):
                        ch(nc.vector.max(top[:, h, 8:16], left[:, h, :]))
                    ch.wait()
                    for h in range(PH):
                        ch(nc.vector.max_index(pos[:, h, 8:16], top[:, h, 8:16], left[:, h, :]))
                    ch.wait()
                    ch.then(nc.vector.tensor_copy(posf[:, :, :], pos[:, :, :]))
                    ch.then(nc.vector.tensor_copy(tot[:, 0, :].unsqueeze(2), top[:, :, 0:1]))
                    ch.then(nc.vector.tensor_tensor(top[:, :, :], top[:, :, :],
                                                    tot[:, 0, :].unsqueeze(2).broadcast_to([P, PH, PK]), ALU.subtract))
                    dve.nop().then_inc(k.sq_ready.sem, 1)
                    for h in range(PH):
                        shape = [P, PK, NCAND]
                        ch(nc.vector.tensor_tensor(hot[:, h, :, :], posf[:, h, :].unsqueeze(2).broadcast_to(shape),
                                                   k.const[:, C_IOTA][:, 0:NCAND].unsqueeze(1).broadcast_to(shape), ALU.is_equal))
                    ch.wait()
                    for h in range(PH):
                        shape = [P, PK, NCAND]
                        ch(nc.vector.tensor_tensor(hot[:, h, :, :], hot[:, h, :, :],
                                                   code[:, h, :].unsqueeze(1).broadcast_to(shape), ALU.mult))
                    ch.wait()
                    ch.then(nc.vector.tensor_reduce(picked[:, tt, 0, :], hot[:, :, :, :].rearrange("p h k n -> p (h k) n"),
                                                    AX.X, ALU.add))
                    ch.then(nc.vector.tensor_copy(whole[:, 0, :], picked[:, tt, 0, :]))
                    ch.then(nc.vector.tensor_scalar(whole[:, 1, :], whole[:, 0, :], NKEYS - 1, None, ALU.bitwise_and))
                    ch.then(nc.vector.tensor_copy(picked[:, tt, 1, :], whole[:, 1, :]))
                    ch.then(nc.vector.tensor_scalar(whole[:, 1, :], whole[:, 0, :], 7, None, ALU.logical_shift_right))
                    ch.then(nc.vector.tensor_copy(picked[:, tt, 0, :], whole[:, 1, :]))
                    dve.wait_ge(k.weights_ready.sem, k.weights_ready.at(tt + 1))
                    gv = picked[:, tt, 2, :].rearrange("p (h k) -> p h k", k=PK)
                    ch.then(nc.vector.tensor_reduce(tot[:, 0, :], gv, AX.X, ALU.add))
                    ch.then(nc.vector.reciprocal(tot[:, 1, :], tot[:, 0, :]))
                    ch.wait()
                    nc.vector.tensor_tensor(gv, gv, tot[:, 1, :].unsqueeze(2).broadcast_to([P, PH, PK]), ALU.mult)\
                        .then_inc(k.probs_ready.sem, 1)

            @block.scalar
            def _(act):
                for tt in range(TT):
                    act.wait_ge(k.sq_ready.sem, k.sq_ready.at(tt + 1))
                    nc.scalar.activation(picked[:, tt, 2, :], top[:, :, :].rearrange("p h k -> p (h k)"), ACT.Exp)\
                        .then_inc(k.weights_ready.sem, 1)
                    act.wait_ge(k.tile_ready.sem, k.tile_ready.at(tt + 1))
                    nc.scalar.activation(k.choice[:, :, tt * P:(tt + 1) * P],
                                         k.bank[tt][:, 0:3 * P].rearrange("p (a t) -> p a t", a=3), ACT.Copy)

            @block.tensor
            def _(pe):
                for tt in range(TT):
                    pe.wait_ge(k.probs_ready.sem, k.probs_ready.at(tt + 1))
                    for a in range(3):
                        ins = nc.tensor.transpose(k.bank[tt][:, a * P:(a + 1) * P], picked[:, tt, a, :], k.const[:, C_ID])
                    ins.then_inc(k.tile_ready.sem, 1)
        for sig in (k.sq_ready, k.weights_ready, k.tile_ready, k.probs_ready):
            sig.advance(TT)


def peer_gates(k, gates):
    nc = k.nc
    GROUP = 4
    BUF = 4
    ngroups = TOK // GROUP
    with ExitStack() as ctx:
        first = ctx.enter_context(nc.sbuf_tensor(k.name("first_hot"), [P, BUF, GROUP, NKEYS], F32))
        second = ctx.enter_context(nc.sbuf_tensor(k.name("second_hot"), [P, BUF, GROUP, NKEYS], F32))
        iota = k.const[:, C_IOTA]
        hot, used, emptied = k.probs_ready, k.tile_ready, k.act_emptied
        with nc.Block() as block:
            @block.vector
            def _(dve):
                def group(g0, it, b):
                    dve.wait_ge(used.sem, g0 + (used.base + b - BUF + 1))
                    for q in range(GROUP):
                        t = g0 * GROUP + (b * GROUP + q)
                        col = lambda a: k.choice[:, a, bass.ds(t, 1)]
                        nc.vector.tensor_scalar(second[:, b, q, :], iota, col(1), None, ALU.is_equal)
                        ins = nc.vector.tensor_scalar(first[:, b, q, :], iota, col(0), col(2), ALU.is_equal, ALU.mult)
                    ins.then_inc(hot.sem, 1)
                rounds(dve, ngroups, BUF, group)

            @block.tensor
            def _(pe):
                def group(g0, it, b):
                    pe.wait_ge(hot.sem, g0 + (hot.base + b + 1))
                    pe.wait_ge(emptied.sem, g0 + (emptied.base + b - BUF + 1))
                    for q in range(GROUP):
                        ins = nc.tensor.matmul(k.bank[b][:, q * P:(q + 1) * P], second[:, b, q, :], first[:, b, q, :],
                                               start=True, stop=True)
                    ins.then_inc(used.sem, 1)
                rounds(pe, ngroups, BUF, group)

            @block.scalar
            def _(act):
                def group(g0, it, b):
                    act.wait_ge(used.sem, g0 + (used.base + b + 1))
                    nc.scalar.activation(gates[:, :, bass.ds(g0 * GROUP + b * GROUP, GROUP)],
                                         k.bank[b][:, :].rearrange("p (q n) -> p n q", q=GROUP), ACT.Copy)\
                        .then_inc(emptied.sem, 1)
                rounds(act, ngroups, BUF, group)
    for sig in (hot, used, emptied):
        sig.advance(ngroups)


def peer_experts(k, gates, gelu, gate):
    nc = k.nc
    NB = NKEYS
    with ExitStack() as ctx:
        act_out = ctx.enter_context(nc.sbuf_tensor(k.name("expert_act"), [P, 2, TOK], F32))
        coef = ctx.enter_context(nc.sbuf_tensor(k.name("coef"), [P, 2, TOK], F32))
        pre, geld, weighed, summed = k.qk_ready, k.act_emptied, k.probs_ready, k.tile_ready
        a = k.chunk
        with nc.Block() as block:
            @block.sync
            def _(sp):
                refill(k, sp, NB, k.w_used, 1)

            @block.tensor
            def _(pe):
                def up(e0, it, j):
                    slot = chunk_wait(k, pe, it, j)
                    pe.wait_ge(geld.sem, e0 + (geld.base + j - 1))
                    w = slot.rearrange("p (k n) -> p k n", n=P)
                    for kk in range(KD):
                        ins = nc.tensor.matmul(k.bank[j % 2][:, 0:TOK], w[:, kk, :], k.h[:, kk, 0:TOK],
                                               start=kk == 0, stop=kk == KD - 1)
                    ins.then_inc(pre.sem, 1)

                def down(e0, j, stop):
                    slot = k.ring[:, (a + j) % SLOTS, :]
                    pe.wait_ge(weighed.sem, e0 + (weighed.base + j + 1))
                    for i in range(KD):
                        ins = nc.tensor.matmul(k.bank[4 + i // 2][:, (i % 2) * TOK:(i % 2 + 1) * TOK],
                                               slot[:, D + i * P:D + (i + 1) * P], coef[:, j % 2, :],
                                               start=False, stop=stop, skip_group_check=True)
                    ins.then_inc(k.w_used.sem, 1)

                pe.wait_ge(k.dve_step.sem, k.dve_step.at(1))
                for q in range(4):
                    nc.tensor.matmul(k.bank[4 + q][:, :], coef[:, 0, 0:P], coef[:, :, :].rearrange("p a t -> p (a t)"),
                                     start=True, stop=False, skip_group_check=True).then_inc(summed.sem, 1)
                up(0, 0, 0)
                with pe.Fori(0, NB // SLOTS - 1) as it:
                    for j in range(SLOTS):
                        up(it * SLOTS, it, j + 1)
                        down(it * SLOTS, j, False)
                last = NB // SLOTS - 1
                for j in range(SLOTS):
                    if j + 1 < SLOTS:
                        up(last * SLOTS, last, j + 1)
                    down(last * SLOTS, j, j == SLOTS - 1)

            @block.scalar
            def _(act):
                def one(e0, it, j):
                    act.wait_ge(pre.sem, e0 + (pre.base + j + 1))
                    act.wait_ge(weighed.sem, e0 + (weighed.base + j - 1))
                    nc.scalar.activation(act_out[:, j % 2, :], k.bank[j % 2][:, 0:TOK], gelu).then_inc(geld.sem, 1)
                rounds(act, NB, SLOTS, one)

            @block.vector
            def _(dve):
                nc.vector.memset(coef[:, :, :], 0.0).then_inc(k.dve_step.sem, 1)
                dve.wait_ge(summed.sem, summed.at(4))

                def one(e0, it, j):
                    dve.wait_ge(geld.sem, e0 + (geld.base + j + 1))
                    dve.wait_ge(k.w_used.sem, e0 + (k.w_used.base + j - 1))
                    nc.vector.tensor_tensor(coef[:, j % 2, :], act_out[:, j % 2, :],
                                            gates[:, bass.ds(e0 + j, 1), :].rearrange("p a t -> p (a t)"), ALU.mult)\
                        .then_inc(weighed.sem, 1)
                rounds(dve, NB, SLOTS, one)
                dve.wait_ge(k.w_used.sem, k.w_used.at(NB))
                for i in range(KD):
                    x = k.x[:, i, META:]
                    ps = k.bank[4 + i // 2][:, (i % 2) * TOK:(i % 2 + 1) * TOK]
                    if gate is None:
                        nc.vector.tensor_tensor(x, ps, x, ALU.add)
                    else:
                        nc.vector.scalar_tensor_tensor(x, ps, gate[:, i:i + 1], x, ALU.mult, ALU.add)
    k.dve_step.advance(1)
    for sig in (pre, geld, weighed, k.w_used):
        sig.advance(NB)
    summed.advance(4)
    k.chunk += NB


def s5_branch(k, ux, mixed, zg):
    nc = k.nc
    HG = S5G // 2
    N2 = 2 * S5N
    with ExitStack() as ctx:
        sb = lambda n, s, d=F32: ctx.enter_context(nc.sbuf_tensor(k.name(n), s, d))
        par = sb("s5_par", [P, 3, S5G])
        rad = sb("s5_radius", [P, S5G])
        phs = sb("s5_phase", [P, 2, S5G])
        tmp = sb("s5_tmp", [P, 8, S5G])
        tmpi = sb("s5_tmpi", [P, S5G], I32)
        cmat = sb("s5_c", [P, 2, S5G, S5C])
        cfold = sb("s5_cfold", [P, 2, S5G, S5C])
        y = sb("s5_y", [P, 4, TOK])
        re, im = slice(0, S5N), slice(S5N, 2 * S5N)
        load = k.s5_dma
        with nc.Block() as block:
            @block.gpsimd
            def _(pool):
                pool.dma_start(par[:, :, :], k.args["s5_par"]).then_inc(load, 16)
                pool.dma_start(cmat[:, :, :, :], k.args["s5_c"]).then_inc(load, 16)

            @block.vector
            def _(dve):
                ch = Chain(dve, k.dve_step)
                T = lambda i: tmp[:, i, :]
                dve.wait_ge(load, 32)
                dve.wait_ge(k.recip_ready.sem, k.recip_ready.at(1))
                ch.then(nc.vector.tensor_tensor(T(1), par[:, 0, :], T(0), ALU.mult))
                ch.then(nc.vector.tensor_tensor(T(2), par[:, 1, :], T(0), ALU.mult))
                turn = 2 * math.pi
                p1 = float(np.float32(round(turn * 256) / 256))
                p2 = float(np.float32(round((turn - p1) * 2 ** 20) / 2 ** 20))
                p3 = float(np.float32(turn - p1 - p2))
                ch.then(nc.vector.tensor_scalar(T(3), T(2), 1 / turn, None, ALU.mult))
                ch.then(nc.vector.tensor_copy(tmpi[:, :], T(3)))
                ch.then(nc.vector.tensor_copy(T(3), tmpi[:, :]))
                for part in (p1, p2, p3):
                    ch.then(nc.vector.scalar_tensor_tensor(T(2), T(3), -part, T(2), ALU.mult, ALU.add))
                for sign in (1.0, -1.0):
                    ch.then(nc.vector.tensor_scalar(T(3), T(2), sign, math.pi, ALU.mult, ALU.is_gt))
                    ch.then(nc.vector.scalar_tensor_tensor(T(2), T(3), -sign * turn, T(2), ALU.mult, ALU.add))
                ch.then(nc.vector.tensor_scalar(T(2), T(2), math.pi, -math.pi, ALU.min, ALU.max))
                nc.vector.tensor_scalar(T(1), T(1), 0.5, None, ALU.mult).then_inc(k.sq_ready.sem, 1)
                dve.wait_ge(k.recip_ready.sem, k.recip_ready.at(4))
                ch.then(nc.vector.tensor_scalar(T(4), T(1), -1.0, 1.0, ALU.mult, ALU.add))
                ch.then(nc.vector.reciprocal(T(5), T(4)))
                ch.then(nc.vector.scalar_tensor_tensor(T(4), T(1), 2.0, T(5), ALU.mult, ALU.mult))
                ch.then(nc.vector.tensor_scalar(rad[:, :], T(4), 1.0, None, ALU.add))
                ch.then(nc.vector.tensor_tensor(T(5), T(3), T(3), ALU.mult))
                ch.then(nc.vector.tensor_scalar(phs[:, 0, :], T(5), -2.0, 1.0, ALU.mult, ALU.add))
                ch.then(nc.vector.tensor_tensor(T(4), T(4), phs[:, 0, :], ALU.mult))
                ch.then(nc.vector.scalar_tensor_tensor(T(4), T(5), -2.0, T(4), ALU.mult, ALU.add))
                ch.then(nc.vector.tensor_tensor(T(5), rad[:, :], phs[:, 1, :], ALU.mult))
                ch.then(nc.vector.tensor_tensor(T(0), par[:, 0, :], par[:, 0, :], ALU.mult))
                ch.then(nc.vector.tensor_tensor(T(1), par[:, 1, :], par[:, 1, :], ALU.mult))
                ch.then(nc.vector.tensor_tensor(T(0), T(0), T(1), ALU.add))
                ch.then(nc.vector.reciprocal(T(1), T(0)))
                ch.then(nc.vector.tensor_tensor(T(2), T(4), par[:, 0, :], ALU.mult))
                ch.then(nc.vector.tensor_tensor(T(3), T(5), par[:, 1, :], ALU.mult))
                ch.then(nc.vector.tensor_tensor(T(2), T(2), T(3), ALU.add))
                ch.then(nc.vector.tensor_tensor(T(6), T(2), T(1), ALU.mult))
                ch.then(nc.vector.tensor_tensor(T(2), T(5), par[:, 0, :], ALU.mult))
                ch.then(nc.vector.tensor_tensor(T(3), T(4), par[:, 1, :], ALU.mult))
                ch.then(nc.vector.tensor_tensor(T(2), T(2), T(3), ALU.subtract))
                ch.then(nc.vector.tensor_tensor(T(7), T(2), T(1), ALU.mult))
                fr = T(6).unsqueeze(2).broadcast_to([P, S5G, S5C])
                fi = T(7).unsqueeze(2).broadcast_to([P, S5G, S5C])
                cr, ci = cmat[:, 0, :, :], cmat[:, 1, :, :]
                ch.then(nc.vector.tensor_tensor(cfold[:, 0, :, :], cr, fr, ALU.mult))
                ch.then(nc.vector.tensor_tensor(cfold[:, 1, :, :], ci, fi, ALU.mult))
                ch.then(nc.vector.tensor_tensor(cfold[:, 0, :, :], cfold[:, 0, :, :], cfold[:, 1, :, :], ALU.subtract))
                ch.then(nc.vector.tensor_tensor(cfold[:, 1, :, :], cr, fi, ALU.mult))
                ch.then(nc.vector.tensor_tensor(cr, ci, fr, ALU.mult))
                ch.then(nc.vector.tensor_tensor(cmat[:, 1, :, :], cfold[:, 1, :, :], cr, ALU.add))
                ch.then(nc.vector.tensor_copy(cmat[:, 0, :, :], cfold[:, 0, :, :]))
                ch(nc.vector.tensor_scalar(cfold[im, 0, :, :], cmat[im, 1, :, :], -1.0, None, ALU.mult))
                ch(nc.vector.tensor_scalar(cfold[re, 1, :, :], cmat[re, 1, :, :], -1.0, None, ALU.mult))
                ch(nc.vector.tensor_scalar(cfold[im, 1, :, :], cmat[im, 0, :, :], -1.0, None, ALU.mult))

            @block.scalar
            def _(act):
                act.wait_ge(load, 32)
                nc.scalar.activation(tmp[:, 0, :], par[:, 2, :], ACT.Exp).then_inc(k.recip_ready.sem, 1)
                act.wait_ge(k.sq_ready.sem, k.sq_ready.at(1))
                nc.scalar.activation(phs[:, 1, :], tmp[:, 2, :], ACT.Sin).then_inc(k.recip_ready.sem, 1)
                nc.scalar.activation(tmp[:, 3, :], tmp[:, 2, :], ACT.Sin, scale=0.5).then_inc(k.recip_ready.sem, 1)
                nc.scalar.activation(tmp[:, 1, :], tmp[:, 1, :], ACT.Tanh).then_inc(k.recip_ready.sem, 1)
        k.recip_ready.advance(4)
        k.sq_ready.advance(1)

        for half in range(2):
            s5_half(k, half, ux, rad, phs, cfold, y)

        with nc.Block() as block:
            @block.scalar
            def _(act):
                nc.scalar.activation(y[:, :, :], y[:, :, :], ACT.Gelu_apprx_tanh)
        sg = sb("s5_gate", [P, 4, TOK])
        bias = k.vec("ssm_b_glu_2")
        linear_t(k, 4, 4, lambda kk: y[:, kk, :], TOK,
                 lambda name, i, ps: nc.scalar.activation(sg[:, i, :], ps, ACT.Sigmoid, bias=bias[:, i:i + 1]), who="act")
        with nc.Block() as block:
            @block.vector
            def _(dve):
                nc.vector.tensor_tensor(y[:, :, :], y[:, :, :], sg[:, :, :], ALU.mult)
        linear_t(k, KD, 4, lambda kk: y[:, kk, :], TOK,
                 lambda name, i, ps: nc.vector.tensor_tensor(mixed[:, i, :], ps, zg[:, 8 + i, :], ALU.mult), who="dve")


def s5_half(k, half, ux, rad, phs, cfold, y):
    nc = k.nc
    HG = S5G // 2
    g0 = half * HG
    with ExitStack() as ctx:
        sb = lambda n, s, d=F32: ctx.enter_context(nc.sbuf_tensor(k.name(n), s, d))
        bmat = sb("s5_b", [P, 2, 2 * S5N])
        bswap = sb("s5_bswap", [P, 2, 2 * S5N])
        bgrp = sb("s5_bgrp", [P, 2, HG, 2 * S5N])
        cgrp = sb("s5_cgrp", [P, 2, HG, P])
        with ExitStack() as ctx2:
            rot = sb("s5_rot", [P, 2, HG, TALL])
            t2 = ctx2.enter_context(nc.sbuf_tensor(k.name("s5_t2"), [P, HG, P], F32))
            pw = ctx2.enter_context(nc.sbuf_tensor(k.name("s5_pw"), [P, 4, HG], F32))
            with nc.Block() as block:
                @block.gpsimd
                def _(pool):
                    pool.dma_start(bmat[:, :, :], k.args["s5_b"][half, :, :, :]).then_inc(k.s5_dma, 16)
                    pool.memset(cgrp[:, :, :, :], 0.0).then_inc(k.pool_step.sem, 1)
                    pool.wait_ge(k.pool_step.sem, k.pool_step.at(1))
                    for j in range(8):
                        ins = nc.gpsimd.tensor_copy(cgrp[:, :, j::8, S5C * j:S5C * (j + 1)], cfold[:, :, g0 + j:g0 + HG:8, :])
                        ins.then_inc(k.pool_step.sem, 1)

                @block.vector
                def _(dve):
                    ch = Chain(dve, k.dve_step)
                    dve.wait_ge(k.s5_dma, 48 + 16 * half)
                    ch(nc.vector.tensor_copy(bswap[:, :, 0:S5N], bmat[:, :, S5N:]))
                    ch(nc.vector.tensor_scalar(bswap[:, :, S5N:], bmat[:, :, 0:S5N], -1.0, None, ALU.mult))
                    ch.wait()
                    for j in range(8):
                        for n, src in enumerate((bmat, bswap)):
                            ch(nc.vector.tensor_scalar(bgrp[:, n, j::8, :], src[:, :, :], k.const[:, C_GRP][:, j:j + 1],
                                                       None, ALU.mult))
                    cos, sin = rot[:, 0, :, :], rot[:, 1, :, :]
                    ch(nc.vector.memset(cos[:, :, 0:1], 1.0))
                    ch(nc.vector.memset(sin[:, :, 0:1], 0.0))
                    ch.then(nc.vector.tensor_copy(pw[:, 0:2, :], phs[:, :, g0:g0 + HG]))
                    n = 1
                    while n < TALL:
                        m = min(n, TALL - n)
                        shape = [P, HG, m]
                        pc = pw[:, 0, :].unsqueeze(2).broadcast_to(shape)
                        ps = pw[:, 1, :].unsqueeze(2).broadcast_to(shape)
                        c0, s0, c1, s1 = cos[:, :, 0:m], sin[:, :, 0:m], cos[:, :, n:n + m], sin[:, :, n:n + m]
                        ch(nc.vector.tensor_tensor(c1, c0, pc, ALU.mult))
                        ch(nc.vector.tensor_tensor(s1, s0, pc, ALU.mult))
                        ch.then(nc.vector.tensor_tensor(t2[:, :, 0:m], s0, ps, ALU.mult))
                        ch.then(nc.vector.tensor_tensor(c1, c1, t2[:, :, 0:m], ALU.subtract))
                        ch.then(nc.vector.tensor_tensor(t2[:, :, 0:m], c0, ps, ALU.mult))
                        ch(nc.vector.tensor_tensor(s1, s1, t2[:, :, 0:m], ALU.add))
                        ch(nc.vector.tensor_tensor(pw[:, 2, :], pw[:, 1, :], pw[:, 1, :], ALU.mult))
                        ch.then(nc.vector.tensor_tensor(pw[:, 3, :], pw[:, 1, :], pw[:, 0, :], ALU.mult))
                        ch(nc.vector.tensor_scalar(pw[:, 0, :], pw[:, 2, :], -2.0, 1.0, ALU.mult, ALU.add))
                        ch.then(nc.vector.tensor_scalar(pw[:, 1, :], pw[:, 3, :], 2.0, None, ALU.mult))
                        n *= 2
            k.pool_step.advance(9)
        tin = sb("s5_tin", [P, 2, 2, TALL])
        z = sb("s5_z", [P, 2, TALL])
        vv = sb("s5_v", [P, 2, 2, TALL])
        bu, bused, scanned, rotated = k.qk_ready, k.probs_ready, k.weights_ready, k.trans_ready
        with nc.Block() as block:
            @block.tensor
            def _(pe):
                def inputs(g):
                    pe.wait_ge(bused.sem, bused.at(g - 1))
                    for n in range(2):
                        ins = nc.tensor.matmul(k.bank[2 * (g % 2) + n][:, 0:TALL], bgrp[:, n, g, :],
                                               ux[:, 2 * half + g // 8, :], start=True, stop=True)
                    ins.then_inc(bu.sem, 1)

                inputs(0)
                for g in range(HG):
                    if g + 1 < HG:
                        inputs(g + 1)
                    pe.wait_ge(rotated.sem, rotated.at(2 * g + 2))
                    for n in range(2):
                        ins = nc.tensor.matmul(k.bank[4 + g // 8][:, 0:TOK], cgrp[:, n, g, :], vv[:, g % 2, n, META:],
                                               start=g % 8 == 0 and n == 0, stop=g % 8 == 7 and n == 1)
                    ins.then_inc(k.tile_ready.sem, 1)

            @block.vector
            def _(dve):
                ch = Chain(dve, k.dve_step)
                for g in range(HG):
                    b = g % 2
                    dve.wait_ge(bu.sem, bu.at(g + 1))
                    ch(nc.vector.tensor_tensor(tin[:, b, 0, :], k.bank[2 * b][:, 0:TALL], rot[:, 0, g, :], ALU.mult))
                    nc.vector.tensor_tensor(tin[:, b, 1, :], k.bank[2 * b + 1][:, 0:TALL], rot[:, 1, g, :], ALU.mult)\
                        .then_inc(bused.sem, 1)
                    dve.wait_ge(bused.sem, bused.at(g + 1))
                    ch.then(nc.vector.tensor_tensor(tin[:, b, 0, :], tin[:, b, 0, :], tin[:, b, 1, :], ALU.add))
                    dve.wait_ge(rotated.sem, rotated.at(2 * g - 2))
                    nc.vector.tensor_tensor_scan(z[:, b, :], rad[:, g0 + g:g0 + g + 1].broadcast_to([P, TALL]),
                                                 tin[:, b, 0, :], 0.0, ALU.mult, ALU.add).then_inc(scanned.sem, 1)
                dve.wait_ge(k.tile_ready.sem, k.tile_ready.at(HG))
                for c in range(2):
                    ct = 2 * half + c
                    nc.vector.scalar_tensor_tensor(y[:, ct, :], ux[:, ct, META:], k.vec("ssm_d_2")[:, ct:ct + 1],
                                                   k.bank[4 + c][:, 0:TOK], ALU.mult, ALU.add)

            @block.gpsimd
            def _(pool):
                for g in range(HG):
                    b = g % 2
                    pool.wait_ge(scanned.sem, scanned.at(g + 1))
                    pool.wait_ge(k.tile_ready.sem, k.tile_ready.at(g - 1))
                    for n in range(2):
                        nc.gpsimd.tensor_tensor(vv[:, b, n, :], z[:, b, :], rot[:, n, g, :], ALU.mult)\
                            .then_inc(rotated.sem, 1)
        for sig in (bu, bused, scanned, k.tile_ready):
            sig.advance(HG)
        rotated.advance(2 * HG)


def mlstm_branch(k, ux, mixed, zg):
    nc = k.nc
    xm = ux[:, 4:12, :]
    with ExitStack() as ctx:
        sb = lambda n, s, d=F32: ctx.enter_context(nc.sbuf_tensor(k.name(n), s, d))
        xc = sb("ml_xc", [P, KD, TALL])
        qkv = sb("ml_qkv", [P, 3 * KD, TALL])
        vn = sb("ml_v", [P, 3, D])
        ht = sb("ml_h", [P, KD, TOK])
        wif = sb("ml_wif", [P, 3 * KD, 2 * MH])
        bif = sb("ml_bif", [MH, 2])
        sel = sb("ml_sel", [MH, MH, P])
        rows = sb("ml_rows", [MH, 8, TALL])
        wcol = sb("ml_wcol", [P, 3, MH])
        cw, cb = k.vec("ml_conv_w_2"), k.vec("ml_conv_b_2")
        with ExitStack() as ctx2:
            bd = ctx2.enter_context(nc.sbuf_tensor("ml_bd", [P, 3 * KD, P], F32))
            wbd = ctx2.enter_context(nc.sbuf_tensor("ml_wbd", [P, 3 * KD, 4], F32))
            with nc.Block() as block:
                @block.gpsimd
                def _(pool):
                    for dst, name in ((wbd[:, :, :], "ml_bd"), (wif[:, :, :], "ml_wif"), (bif[:, :], "ml_bif"),
                                      (sel[:, :, :], "sel")):
                        pool.dma_start(dst, k.args[name]).then_inc(k.ml_dma, 16)

                @block.vector
                def _(dve):
                    ch = Chain(dve, k.dve_step)
                    for i in range(KD):
                        ch(nc.vector.tensor_scalar(xc[:, i, :], xm[:, i, :], cw[:, 24 + i:25 + i], cb[:, i:i + 1],
                                                   ALU.mult, ALU.add))
                    ch.wait()
                    for j in range(3):
                        for i in range(KD):
                            back = 3 - j
                            ch(nc.vector.scalar_tensor_tensor(xc[:, i, back:], xm[:, i, 0:TALL - back],
                                                              cw[:, 8 * j + i:8 * j + i + 1], xc[:, i, back:],
                                                              ALU.mult, ALU.add))
                        ch.wait()
                    dve.nop().then_inc(k.sq_ready.sem, 1)
                    dve.wait_ge(k.ml_dma, 64)
                    ch.then(nc.vector.tensor_tensor(
                        bd[:, :, :].rearrange("p m (n d) -> p m n d", d=4),
                        wbd[:, :, :].unsqueeze(2).broadcast_to([P, 3 * KD, 32, 4]),
                        k.const[:, C_BD].rearrange("p (n d) -> p n d", d=4).unsqueeze(1).broadcast_to([P, 3 * KD, 32, 4]),
                        ALU.mult))

                @block.scalar
                def _(act):
                    act.wait_ge(k.sq_ready.sem, k.sq_ready.at(1))
                    nc.scalar.activation(xc[:, :, :], xc[:, :, :], ACT.Silu)
            k.sq_ready.advance(1)

            tok_tiles = ((0, META), (META, META + P), (META + P, TALL))
            with nc.Block() as block:
                @block.tensor
                def _(pe):
                    for m in range(3 * KD):
                        src = xc[:, m % KD, :] if m < 2 * KD else xm[:, m % KD, :]
                        emptied, half = (k.act_emptied, k.dve_emptied)[m % 2], m // 2
                        pe.wait_ge(emptied.sem, emptied.at(half - 1))
                        nc.tensor.matmul(k.bank[m % 4][:, 0:TALL], bd[:, m, :], src, start=True, stop=True)\
                            .then_inc(k.tile_ready.sem, 1)
                    for n in range(6):
                        (t0, t1), side = tok_tiles[n // 2], n % 2
                        emptied = (k.act_emptied, k.dve_emptied)[side]
                        if n >= 4:
                            pe.wait_ge(emptied.sem, emptied.at(12 + n // 2 - 1))
                        for i in range(4):
                            ins = nc.tensor.matmul(k.bank[4 + n % 4][0:t1 - t0, i * P:(i + 1) * P], xm[:, 4 * side + i, t0:t1],
                                                   bd[:, 2 * KD + 4 * side + i, :], start=True, stop=True)
                        ins.then_inc(k.tile_ready.sem, 1)

                def emptying(eng, side, copy, sig):
                    for m in range(side, 3 * KD, 2):
                        eng.wait_ge(k.tile_ready.sem, k.tile_ready.at(m + 1))
                        copy(qkv[:, m, :], k.bank[m % 4][:, 0:TALL]).then_inc(sig.sem, 1)
                    for n in range(side, 6, 2):
                        (t0, t1) = tok_tiles[n // 2]
                        eng.wait_ge(k.tile_ready.sem, k.tile_ready.at(3 * KD + n + 1))
                        copy(vn[0:t1 - t0, n // 2, side * 512:(side + 1) * 512], k.bank[4 + n % 4][0:t1 - t0, :])\
                            .then_inc(sig.sem, 1)

                @block.scalar
                def _(act):
                    emptying(act, 0, lambda o, i: nc.scalar.activation(o, i, ACT.Copy), k.act_emptied)

                @block.vector
                def _(dve):
                    emptying(dve, 1, lambda o, i: nc.vector.tensor_copy(o, i), k.dve_emptied)
            k.tile_ready.advance(30)
            k.act_emptied.advance(15)
            k.dve_emptied.advance(15)

        R = lambda i: rows[:, i, :]
        with nc.Block() as block:
            @block.tensor
            def _(pe):
                for side in range(2):
                    for m in range(3 * KD):
                        ins = nc.tensor.matmul(k.bank[side][0:MH, 0:TALL], wif[:, m, side * MH:(side + 1) * MH],
                                               qkv[:, m, :], start=m == 0, stop=m == 3 * KD - 1)
                    ins.then_inc(k.tile_ready.sem, 1)
                pe.wait_ge(k.dve_emptied.sem, k.dve_emptied.at(1))
                for n, (t0, t1) in enumerate(((0, META), (META, META + P), (META + P, TALL))):
                    ins = nc.tensor.transpose(k.bank[2][0:t1 - t0, n * MH:(n + 1) * MH], R(4)[:, t0:t1],
                                              k.const[0:MH, 0:MH])
                ins.then_inc(k.tile_ready.sem, 1)

            @block.vector
            def _(dve):
                ch = Chain(dve, k.dve_step)
                dve.wait_ge(k.tile_ready.sem, k.tile_ready.at(2))
                ch(nc.vector.memset(R(7), 1.0))
                ch(nc.vector.tensor_scalar(R(0), k.bank[0][0:MH, 0:TALL], bif[:, 0:1], None, ALU.add))
                ch.then(nc.vector.tensor_scalar(R(1), k.bank[1][0:MH, 0:TALL], bif[:, 1:2], None, ALU.add))
                nc.vector.scalar_tensor_tensor(R(2), R(1), -1.0, R(1), ALU.mult, ALU.max).then_inc(k.sq_ready.sem, 1)
                ch.then(nc.vector.tensor_scalar(R(1), R(1), 0.0, None, ALU.min))
                dve.wait_ge(k.recip_ready.sem, k.recip_ready.at(1))
                ch.then(nc.vector.tensor_tensor(R(1), R(1), R(3), ALU.subtract))
                ch.then(nc.vector.tensor_tensor_scan(R(2), R(7), R(1), 0.0, ALU.mult, ALU.add))
                nc.vector.tensor_tensor(R(4), R(0), R(2), ALU.subtract).then_inc(k.dve_emptied.sem, 1)
                dve.wait_ge(k.dve_emptied.sem, k.dve_emptied.at(1))
                ch.then(nc.vector.tensor_tensor_scan(R(5), R(4), R(4), 0.0, ALU.max, ALU.max))
                ch.then(nc.vector.tensor_tensor(R(6), R(2), R(5), ALU.add))
                ch.then(nc.vector.tensor_scalar(R(6), R(6), -1.0, None, ALU.mult))
                dve.wait_ge(k.tile_ready.sem, k.tile_ready.at(3))
                ch(nc.vector.tensor_copy(wcol[0:META, 0, :], k.bank[2][0:META, 0:MH]))
                ch(nc.vector.tensor_copy(wcol[:, 1:3, :].rearrange("p a h -> p (a h)"), k.bank[2][:, MH:3 * MH]))

            @block.scalar
            def _(act):
                act.wait_ge(k.sq_ready.sem, k.sq_ready.at(1))
                nc.scalar.activation(R(3), R(2), ACT.Exp, scale=-1.0).then_inc(k.act_step.sem, 1)
                act.wait_ge(k.act_step.sem, k.act_step.at(1))
                nc.scalar.activation(R(3), R(3), ACT.Ln, bias=1.0).then_inc(k.recip_ready.sem, 1)
        k.tile_ready.advance(3)
        k.dve_emptied.advance(1)
        k.sq_ready.advance(1)
        k.recip_ready.advance(1)
        k.act_step.advance(1)

        mlstm_heads(k, xc, qkv, vn, sel, rows, wcol, zg, ht)

        def evac(name, i, ps):
            return nc.vector.tensor_tensor(ht_out[:, i, :], ps, zg[:, 16 + i, :], ALU.mult)
        ht_out = sb("ml_out", [P, KD, TOK])
        linear_t(k, KD, KD, lambda kk: ht[:, kk, :], TOK, evac, who="dve")
        with nc.Block() as block:
            @block.vector
            def _(dve):
                nc.vector.tensor_tensor(mixed[:, :, :], mixed[:, :, :], ht_out[:, :, :], ALU.add)


def mlstm_heads(k, xc, qkv, vn, sel, rows, wcol, zg, ht):
    nc = k.nc
    tiles = ((0, META, 0, False), (META, META + P, 0, True), (META + P, TALL, P, True))
    with ExitStack() as ctx:
        sb = lambda n, s, d=F32: ctx.enter_context(nc.sbuf_tensor(k.name(n), s, d))
        later = sb("later", [P, P])
        mb = sb("max_rows", [P, 2, 3, TOK])
        dec = sb("decay", [P, 2, 3, TOK])
        wsc = sb("weighted", [P, 2, 3, TOK])
        floor = sb("floor", [P, 2, TOK])
        den = sb("den", [P, 3, TOK])
        hz = sb("hz", [P, 2, TOK])
        sqh = sb("sqh", [P, 2, TOK])
        with nc.Block() as block:
            @block.tensor
            def _(pe):
                def start(h):
                    pe.wait_ge(k.qk_ready.sem, k.qk_ready.at(h))
                    nc.tensor.matmul(k.bank[0][:, 0:TOK], sel[:, h, :], rows[:, 5, META:], start=True, stop=True)
                    nc.tensor.matmul(k.bank[1][:, 0:TOK], sel[:, h, :], rows[:, 6, META:], start=True, stop=True)\
                        .then_inc(k.tile_ready.sem, 1)
                    for n, (s0, s1, q0, _) in enumerate(tiles):
                        for j in range(2):
                            ins = nc.tensor.matmul(k.bank[2 + n][0:s1 - s0, q0:TOK], qkv[:, KD + 2 * h + j, s0:s1],
                                                   qkv[:, 2 * h + j, META + q0:], start=j == 0, stop=j == 1)
                    ins.then_inc(k.tile_ready.sem, 1)

                start(0)
                for h in range(MH):
                    pe.wait_ge(k.weights_ready.sem, k.weights_ready.at(h + 1))
                    pe.wait_ge(k.probs_ready.sem, k.probs_ready.at(h))
                    for o in range(3):
                        for n, (s0, s1, q0, _) in enumerate(tiles):
                            rowsn = s1 - s0
                            left = k.ones[0:rowsn, :] if o == 2 else vn[0:rowsn, n, h * MDH + o * P:h * MDH + (o + 1) * P]
                            ins = nc.tensor.matmul(k.bank[5 + o][:, q0:TOK], left, wsc[0:rowsn, h % 2, n, q0:],
                                                   start=n == 0, stop=n == 2)
                    ins.then_inc(k.trans_ready.sem, 1)
                    if h + 1 < MH:
                        start(h + 1)
                    pe.wait_ge(k.sq_ready.sem, k.sq_ready.at(h + 1))
                    for o in range(2):
                        ins = nc.tensor.matmul(k.bank[5][:, 256:512], k.ones[:, :], sqh[:, o, :], start=o == 0, stop=o == 1)
                    ins.then_inc(k.trans_ready.sem, 1)

            @block.scalar
            def _(act):
                ch = Chain(act, k.act_step)
                for h in range(MH):
                    b = h % 2
                    act.wait_ge(k.tile_ready.sem, k.tile_ready.at(2 * h + 1))
                    act.wait_ge(k.probs_ready.sem, k.probs_ready.at(h - 1))
                    nc.scalar.activation(floor[:, b, :], k.bank[1][:, 0:TOK], ACT.Exp).then_inc(k.act_emptied.sem, 1)
                    act.wait_ge(k.recip_ready.sem, k.recip_ready.at(2 * h + 1))
                    for n, (s0, s1, q0, _) in enumerate(tiles):
                        r = slice(0, s1 - s0)
                        nc.scalar.activation(dec[r, b, n, q0:], mb[r, b, n, q0:], ACT.Exp, scale=-1.0,
                                             bias=wcol[r, n, h:h + 1]).then_inc(k.act_emptied.sem, 1)
                    act.wait_ge(k.recip_ready.sem, k.recip_ready.at(2 * h + 2))
                    nc.scalar.activation(den[:, 2, :], den[:, 1, :], ACT.Sqrt).then_inc(k.act_emptied.sem, 1)

            @block.vector
            def _(dve):
                ch = Chain(dve, k.dve_step)
                ch.then(nc.vector.tensor_scalar(later[:, :], k.const[:, C_UP], -BIG, BIG, ALU.mult, ALU.add))
                for h in range(MH):
                    b = h % 2
                    dve.wait_ge(k.tile_ready.sem, k.tile_ready.at(2 * h + 1))
                    for n, (s0, s1, q0, masked) in enumerate(tiles):
                        r = slice(0, s1 - s0)
                        if masked:
                            ch(nc.vector.tensor_tensor(mb[:, b, n, q0:q0 + P], k.bank[0][:, q0:q0 + P], later[:, :], ALU.add))
                        if not masked or q0 == 0:
                            q1 = q0 + P if masked else q0
                            ch(nc.vector.tensor_copy(mb[r, b, n, q1:], k.bank[0][r, q1:TOK]))
                    ch.wait()
                    dve.nop().then_inc(k.recip_ready.sem, 1)
                    dve.wait_ge(k.act_emptied.sem, k.act_emptied.at(5 * h + 4))
                    dve.wait_ge(k.tile_ready.sem, k.tile_ready.at(2 * h + 2))
                    for n, (s0, s1, q0, _) in enumerate(tiles):
                        r = slice(0, s1 - s0)
                        ch(nc.vector.scalar_tensor_tensor(wsc[r, b, n, q0:], k.bank[2 + n][r, q0:TOK], MDH ** -0.5,
                                                          dec[r, b, n, q0:], ALU.mult, ALU.mult))
                    ch.wait()
                    dve.nop().then_inc(k.weights_ready.sem, 1)
                    dve.nop().then_inc(k.qk_ready.sem, 1)
                    dve.wait_ge(k.trans_ready.sem, k.trans_ready.at(2 * h + 1))
                    ch.then(nc.vector.tensor_copy(den[:, 1, :], k.bank[7][:, 0:TOK]))
                    ch.then(nc.vector.scalar_tensor_tensor(den[:, 0, :], den[:, 1, :], -1.0, den[:, 1, :], ALU.mult, ALU.max))
                    ch.then(nc.vector.tensor_tensor(den[:, 0, :], den[:, 0, :], floor[:, b, :], ALU.max))
                    ch.then(nc.vector.reciprocal(den[:, 1, :], den[:, 0, :]))
                    for o in range(2):
                        ch(nc.vector.tensor_tensor(hz[:, o, :], k.bank[5 + o][:, 0:TOK], den[:, 1, :], ALU.mult))
                    ch.wait()
                    ch.then(nc.vector.tensor_tensor(hz[:, :, :], hz[:, :, :], zg[:, 2 * h:2 * h + 2, :], ALU.mult))
                    nc.vector.tensor_tensor(sqh[:, :, :], hz[:, :, :], hz[:, :, :], ALU.mult).then_inc(k.sq_ready.sem, 1)
                    dve.wait_ge(k.trans_ready.sem, k.trans_ready.at(2 * h + 2))
                    ch.then(nc.vector.tensor_scalar(den[:, 0, :], k.bank[5][:, 256:512], 1.0 / MDH, EPS, ALU.mult, ALU.add))
                    nc.vector.reciprocal(den[:, 1, :], den[:, 0, :]).then_inc(k.recip_ready.sem, 1)
                    dve.wait_ge(k.act_emptied.sem, k.act_emptied.at(5 * h + 5))
                    ch.then(nc.vector.tensor_tensor(hz[:, :, :], hz[:, :, :],
                                                    den[:, 2:3, :].broadcast_to([P, 2, TOK]), ALU.mult))
                    for o in range(2):
                        i = 2 * h + o
                        ch(nc.vector.tensor_scalar(ht[:, i, :], hz[:, o, :], k.vec("ml_norm_g_2")[:, i:i + 1], None, ALU.mult))
                    ch.wait()
                    for o in range(2):
                        i = 2 * h + o
                        ch(nc.vector.scalar_tensor_tensor(ht[:, i, :], xc[:, i, META:], k.vec("ml_skip_2")[:, i:i + 1],
                                                          ht[:, i, :], ALU.mult, ALU.add))
                    ch.wait()
                    dve.nop().then_inc(k.probs_ready.sem, 1)
    k.tile_ready.advance(2 * MH)
    k.trans_ready.advance(2 * MH)
    k.act_emptied.advance(5 * MH)
    k.recip_ready.advance(2 * MH)
    for sig in (k.weights_ready, k.qk_ready, k.sq_ready, k.probs_ready):
        sig.advance(MH)


SIGNALS = ("w_used", "tile_ready", "act_emptied", "dve_emptied", "dve_step", "act_step", "pool_step", "sq_ready",
           "recip_ready", "qk_ready", "weights_ready", "probs_ready", "trans_ready")


def build(nc, args, out, stop=None):
    k = K()
    k.nc, k.args, k.chunk, k.names = nc, args, 0, {}

    def name(n):
        k.names[n] = k.names.get(n, -1) + 1
        return f"{n}_{k.names[n]}"
    k.name = name
    with ExitStack() as ctx:
        sb = lambda n, s, d=F32: ctx.enter_context(nc.sbuf_tensor(n, s, d))
        k.counters = {n: Signal(ctx.enter_context(nc.semaphore(n))) for n in SIGNALS}
        (k.w_used, k.tile_ready, k.act_emptied, k.dve_emptied, k.dve_step, k.act_step, k.pool_step, k.sq_ready,
         k.recip_ready, k.qk_ready, k.weights_ready, k.probs_ready, k.trans_ready) = (k.counters[n] for n in SIGNALS)
        k.w_loaded = [ctx.enter_context(nc.semaphore(f"w_loaded{i}")) for i in range(SLOTS)]
        k.const_dma, k.x_dma, k.bias_dma, k.s5_dma, k.ml_dma, k.out_dma = (
            ctx.enter_context(nc.semaphore(n)) for n in ("const_dma", "x_dma", "bias_dma", "s5_dma", "ml_dma", "out_dma"))
        k.bank = [ctx.enter_context(nc.psum_tensor(f"bank{i}", [P, 512], F32)) for i in range(BANKS)]
        k.bias_dram = nc.dram_tensor("bias_rows", (P, HEADS, 3 * P), F32, kind="Internal").ap()
        k.ring = sb("ring", [P, SLOTS, CHUNK])
        k.x = sb("x", [P, KD, TALL])
        k.h = sb("h", [P, KD, TALL])
        k.const = sb("const", [P, NCONST])
        k.onehot = sb("onehot", [BUCKETS, 3 * P])
        k.rel = sb("rel", [BUCKETS, HEADS])
        k.ones = sb("ones", [P, P])
        vecs = sb("vecs", [P, NVEC])
        k.vec = lambda n: vecs[:, VEC[n]]
        k.mod = sb("mod", [P, 6 * KD])
        k.gain = sb("gain", [P, 2, KD])
        k.choice = sb("choice", [P, 3, TOK])

        with nc.Block() as block:
            @block.sync
            def _(sp):
                sp.dma_start(vecs[:, :], args["vecs"]).then_inc(k.const_dma, 16)
                for c in range(SLOTS):
                    load_chunk(k, sp, c)

            @block.scalar
            def _(act):
                act.dma_start(k.x[:, :, META:], args["x_t"]).then_inc(k.x_dma, 16)
                act.dma_start(k.x[:, :, 0:META], args["meta_t"]).then_inc(k.x_dma, 16)
                act.dma_start(k.const[:, :], args["const"]).then_inc(k.const_dma, 16)
                act.dma_start(k.onehot[:, :], args["onehot"]).then_inc(k.const_dma, 16)
                act.dma_start(k.rel[:, :], args["rel_bias"]).then_inc(k.const_dma, 16)
                act.wait_ge(k.const_dma, 64)
                act.wait_ge(k.x_dma, 32)

            @block.gpsimd
            def _(pool):
                pool.memset(k.ones[:, :], 1.0)
                for n in SIGNALS:
                    pool.sem_inc(k.counters[n].sem, CREDIT)

        def done(what):
            return stop == what

        def finish(src):
            with nc.Block() as block:
                @block.sync
                def _(sp):
                    sp.dma_start(out, src).then_inc(k.out_dma, 16)
                    sp.wait_ge(k.out_dma, 16)
            if stop is not None:
                with nc.Block() as block:
                    @block.sync
                    def _(sp):
                        for c in range(SLOTS):
                            at = min(k.chunk + c, NCHUNKS - 1)
                            sp.wait_ge(k.w_loaded[at % SLOTS], LOADED[at])

        real = k.x[:, :, META:]
        modulation(k)
        rmsnorm_t(k, real, TOK, k.h[:, :, 0:TOK], k.gain[:, 0, :], k.mod[:, 0:KD])
        if done("norm1"):
            return finish(k.h[:, :, 0:TOK])
        with ExitStack() as ctx1:
            sb1 = lambda n, s: ctx1.enter_context(nc.sbuf_tensor(n, s, F32))
            pt = sb1("proj_t", [P, 36, TOK])
            v = sb1("values", [P, TT, D])
            kit = sb1("ki_t", [P, TOK])
            wi = sb1("wi", [P, 16])
            bias0 = sb1("bias0", [P, HEADS, P])
            bias1 = sb1("bias1", [P, HEADS, 2 * P])
            yt = sb1("y_t", [P, KD, TOK])
            merged = sb1("merged", [P, KD, TOK])
            block1_projections(k, pt, v, kit, wi)
            position_bias(k, bias1)
            index_selection(k, pt, kit, wi, bias0, bias1)
            attentions(k, pt, v, bias0, bias1, yt)
            if done("att"):
                return finish(yt[:, :, :])
            merge1(k, pt, yt, merged)
            linear_t(k, KD, KD, lambda kk: merged[:, kk, :], TOK, add_residual(k, k.mod[:, 2 * KD:3 * KD]), who="dve")
        if done("mix1"):
            return finish(real)
        rmsnorm_t(k, real, TOK, k.h[:, :, 0:TOK], k.gain[:, 1, :], k.mod[:, 3 * KD:4 * KD])
        peer(k, ACT.Gelu, k.mod[:, 5 * KD:6 * KD])
        if done("peer1"):
            return finish(real)
        rmsnorm_t(k, real, TOK, real, k.vec("final_g"), None)
        rmsnorm_t(k, k.x[:, :, :], TALL, k.h[:, :, :], k.vec("norm1_g_2"), None)
        if done("norm2"):
            return finish(k.h[:, :, META:])
        with ExitStack() as ctx1:
            sb1 = lambda n, s: ctx1.enter_context(nc.sbuf_tensor(n, s, F32))
            zg = sb1("z_gates", [P, 24, TOK])
            mixed = sb1("mixed", [P, KD, TOK])
            with ExitStack() as ctx2:
                ux = ctx2.enter_context(nc.sbuf_tensor("ux", [P, 12, TALL], F32))
                linear_t(k, 12, KD, lambda kk: k.h[:, kk, :], TALL, copy_to(k, ux))
                linear_t(k, 24, KD, lambda kk: k.h[:, kk, META:], TOK,
                         lambda name, i, ps: nc.scalar.activation(
                             zg[:, bass.ds(i, 1), :].rearrange("p a n -> p (a n)"), ps, ACT.Sigmoid), who="act")
                s5_branch(k, ux, mixed, zg)
                if done("s5"):
                    return finish(mixed[:, :, :])
                mlstm_branch(k, ux, mixed, zg)
                if done("ml"):
                    return finish(mixed[:, :, :])
            linear_t(k, KD, KD, lambda kk: mixed[:, kk, :], TOK, add_residual(k, None), who="dve")
        if done("mix2"):
            return finish(real)
        rmsnorm_t(k, real, TOK, k.h[:, :, 0:TOK], k.vec("norm2_g_2"), None)
        peer(k, ACT.Gelu_apprx_tanh, None)
        rmsnorm_t(k, real, TOK, k.h[:, :, 0:TOK], k.vec("final_norm_g_2"), None)
        finish(k.h[:, :, 0:TOK])


def peer(k, gelu, gate):
    peer_select(k)
    with ExitStack() as ctx:
        gates = ctx.enter_context(k.nc.sbuf_tensor(k.name("gates"), [P, NKEYS, TOK], F32))
        peer_gates(k, gates)
        peer_experts(k, gates, gelu, gate)


def buckets():
    n = np.maximum(255 - np.arange(3 * P), 0)
    nf = np.maximum(n, 1).astype(np.float32)
    large = 16 + (np.log(nf / np.float32(16)) / np.float32(math.log(8)) * np.float32(16)).astype(np.int32)
    b = np.where(n < 16, n, np.minimum(large, 31))
    return (np.arange(BUCKETS)[:, None] == b[None, :]).astype(np.float32)


def constants():
    i = np.arange(P)
    c = np.zeros((P, NCONST), np.float32)
    c[:, C_ID] = np.eye(P)
    c[:, C_IOTA] = i[None, :]
    c[:, C_LOW] = i[None, :] <= i[:, None]
    c[:, C_STRICT] = i[None, :] < i[:, None]
    c[:, C_UP] = i[None, :] >= i[:, None]
    c[:, C_BD] = i[None, :] // 4 == i[:, None] // 4
    c[:, C_GRP] = np.arange(8)[None, :] == i[:, None] // S5C
    return c


def layout(a):
    a = {n: np.asarray(x) for n, x in a.items()}
    dense = np.zeros((NDENSE, P, CHUNK), np.float32)
    first = lambda name: DENSE_AT[CHUNKS[name][0]]

    def put(name, w):
        nk = w.shape[0] // P
        cols = CHUNK // nk
        c0 = first(name) if isinstance(name, str) else name
        n = w.shape[1] // cols
        dense[c0:c0 + n].reshape(n, P, nk, cols)[:] = w.reshape(nk, P, n, cols).transpose(2, 1, 0, 3)

    put("ada", a["w_ada"][0])
    w = a["w_in"][0]
    o = np.cumsum([0, 512, 512, 512, 512, 64, 8, 512, 512, 512, 1024, 1024])
    part = lambda i: w[:, o[i]:o[i + 1]]
    put("in1", np.concatenate([part(0), part(1), part(3), part(6), part(7), part(9), part(10)], 1))
    put("v1", np.concatenate([part(2), part(8)], 1))
    ki = dense[first("ki")].reshape(P, KD, 256)
    for at, i in ((0, 4), (64, 4), (128, 5)):
        ki[:, :, at:at + part(i).shape[1]] = part(i).reshape(KD, P, -1).transpose(1, 0, 2)
    c0 = first("projab")
    for half in range(2):
        for side, n in enumerate(("w_proj_a", "w_proj_b")):
            put(c0 + 2 * half + side, a[n][0][:, 512 * half:512 * (half + 1)])
    put("out1", a["w_out"][0])
    tables = {}
    for s, wq, keys, u, v in (("1", "peer_wq", "peer_sub_keys", "peer_u", "peer_v"),
                              ("2", "peer_w_q_2", "peer_sub_keys_2", "peer_u_2", "peer_v_2")):
        put("wq" + s, a[wq][0])
        dense[first("keys" + s)] = a[keys][0].reshape(2 * PH, NKEYS, P).transpose(2, 0, 1).reshape(P, CHUNK)
        tables["u" + s] = np.ascontiguousarray(a[u][0].reshape(NKEYS, P, KD, P).transpose(0, 3, 2, 1)).reshape(NKEYS, P, D)
        tables["v" + s] = a[v][0].reshape(NKEYS, P, D)
    put("in2", a["w_in_2"][0])
    put("glu", a["ssm_w_glu_2"][0])
    put("ssmout", a["w_ssm_out_2"][0])
    put("mlout", a["w_ml_out_2"][0])
    put("out2", a["w_out_2"][0])

    vecs = np.empty((P, NVEC), np.float32)
    for n, s in VEC.items():
        vecs[:, s] = a[n].reshape(-1, P).T
    twice = lambda x: np.concatenate([x, x], 0)
    b = np.concatenate([a["ssm_b_re_2"][0].transpose(0, 2, 1), a["ssm_b_im_2"][0].transpose(0, 2, 1)], 2)
    return {
        "dense": dense,
        **tables,
        "vecs": vecs,
        "x_t": np.ascontiguousarray(a["x"][0].T.reshape(KD, P, TOK).transpose(1, 0, 2)),
        "meta_t": np.ascontiguousarray(a["meta_tokens_2"].T.reshape(KD, P, META).transpose(1, 0, 2)),
        "const": constants(),
        "onehot": buckets(),
        "rel_bias": a["rel_bias"],
        "s5_par": np.ascontiguousarray(twice(np.stack(
            [a["ssm_a_re_2"][0].T, a["ssm_a_im_2"][0].T, np.broadcast_to(a["ssm_log_dt_2"][0][None], (S5N, S5G))], 1))),
        "s5_c": np.ascontiguousarray(twice(np.stack(
            [a["ssm_c_re_2"][0].transpose(2, 0, 1), a["ssm_c_im_2"][0].transpose(2, 0, 1)], 1))),
        "s5_b": np.ascontiguousarray(b.reshape(2, 2, P, 2 * S5N).transpose(0, 2, 1, 3)),
        "ml_bd": np.ascontiguousarray(np.stack([a[n][0].reshape(KD, P, 4) for n in ("ml_wq_2", "ml_wk_2", "ml_wv_2")])
                                      .reshape(3 * KD, P, 4).transpose(1, 0, 2)),
        "ml_wif": np.ascontiguousarray(a["ml_w_if_2"][0].reshape(3 * KD, P, 2 * MH).transpose(1, 0, 2)),
        "ml_bif": np.ascontiguousarray(a["ml_b_if_2"][0].reshape(2, MH).T),
        "sel": np.ascontiguousarray(np.broadcast_to(np.eye(MH, dtype=np.float32)[:, :, None], (MH, MH, P))),
    }


def kernel(**inputs):
    import concourse.bacc as bacc
    from concourse.bass_utils import run_bass_kernel_spmd

    nc = bacc.Bacc("TRN2", target_bir_lowering=False, num_devices=1)
    arrays = layout(inputs)
    args = {n: nc.dram_tensor(f"in_{n}", x.shape, F32, kind="ExternalInput").ap() for n, x in arrays.items()}
    out = nc.dram_tensor("out", (P, KD, TOK), F32, kind="ExternalOutput").ap()
    build(nc, args, out)
    r = run_bass_kernel_spmd(nc, [{f"in_{n}": x for n, x in arrays.items()}], core_ids=[0])
    return np.ascontiguousarray(r.results[0]["out"].transpose(1, 0, 2).reshape(D, TOK).T)[None]
```
